# Optimizing a Trainium2 kernel written in Bass

```python
import math
import jax
import jax.numpy as jnp
from jax import lax
import numpy as np

D_MODEL = 2048
BATCH = 1
SEQ = 256
DEPTH = 1

CTX_LEN = 256
GRID_W = 64
MIX_WIDTH = D_MODEL
HYENA_WIDTH = MIX_WIDTH // 2
HYENA_GROUPS = 8
HYENA_PROJ = 3 * HYENA_WIDTH
FILTER_BANDS = 16
FILTER_EMB = 1 + 2 * FILTER_BANDS
FILTER_HIDDEN = 64
FILTER_TARGET = 1e-2
FILTER_FAST_PCT = 0.3
FILTER_SLOW_PCT = 1.5
GLA_HEADS = 8
GLA_DV = (MIX_WIDTH - HYENA_WIDTH) // GLA_HEADS
GLA_DK = GLA_DV // 2
GLA_QK = GLA_HEADS * GLA_DK
GLA_V = GLA_HEADS * GLA_DV
GLA_RANK = 16
GLA_GATE_TAU = 16.0
GLA_CHUNK = 64
GLA_STATE_COLS = GLA_QK + GLA_V + 2 * GLA_RANK
GLA_PROJ = GLA_STATE_COLS + GLA_QK + GLA_V
IN_WIDTH = HYENA_PROJ + GLA_PROJ
D_FF = 5632
NORM_EPS = 1e-6

kernel_name = 'hybrid_hyena_gla_dit_block'

def rmsnorm(x, g):
    x32 = x.astype(jnp.float32)
    y = x32 * lax.rsqrt(jnp.mean(x32 * x32, axis=-1, keepdims=True) + NORM_EPS)
    return (y * g.astype(jnp.float32)).astype(x.dtype)

def adaln_params(cvec, w_mod, b_mod):
    m = jax.nn.silu(cvec) @ w_mod + b_mod
    return jnp.split(m, 6, axis=-1)

def modulate(h, shift, scale):
    return h * (1 + scale) + shift

def dwconv1d(x, w):
    return lax.conv_general_dilated(x, w[:, None, :].astype(x.dtype), (1,), 'SAME',
                                    dimension_numbers=('NWC', 'WIO', 'NWC'),
                                    feature_group_count=x.shape[-1])

def dwconv2d(x, w, rows, cols):
    b, l, ch = x.shape
    y = lax.conv_general_dilated(x.reshape(b, rows, cols, ch), w[:, :, None, :].astype(x.dtype), (1, 1), 'SAME',
                                 dimension_numbers=('NHWC', 'HWIO', 'NHWC'), feature_group_count=ch)
    return y.reshape(b, l, ch)

def hyena_filter(seq_len, w1, b1, freq, w2, b2, w3):
    f32 = jnp.float32
    pos = jnp.arange(seq_len, dtype=f32)
    t = pos / max(seq_len - 1, 1)
    bands = jnp.arange(1, FILTER_BANDS + 1, dtype=f32)
    ang = (2.0 * math.pi / seq_len) * pos[:, None] * bands[None, :]
    z = jnp.concatenate([t[:, None], jnp.cos(ang), jnp.sin(ang)], axis=-1)
    fr = freq.astype(f32)
    h = jnp.sin(fr * (z @ w1.astype(f32) + b1.astype(f32)))
    h = jnp.sin(fr * (h @ w2.astype(f32) + b2.astype(f32)))
    h = h @ w3.astype(f32)
    deltas = jnp.abs(jnp.linspace(math.log(FILTER_TARGET) / FILTER_SLOW_PCT,
                                  math.log(FILTER_TARGET) / FILTER_FAST_PCT, HYENA_WIDTH, dtype=f32))
    decay = jnp.exp(-t[:, None] * deltas[None, :])
    h_fwd = h[:, :HYENA_WIDTH] * decay
    h_bwd = h[:, HYENA_WIDTH:] * decay
    return jnp.concatenate([h_fwd, jnp.zeros((1, HYENA_WIDTH), f32), h_bwd[:0:-1]], axis=0)

def fft_long_conv(u, k2):
    l = u.shape[1]
    uf = jnp.fft.rfft(u.astype(jnp.float32), n=2 * l, axis=1)
    kf = jnp.fft.rfft(k2, n=2 * l, axis=0)
    return jnp.fft.irfft(uf * kf[None], n=2 * l, axis=1)[:, :l].astype(u.dtype)

def hyena_mixer(p, lp):
    b, l, _ = p.shape
    x0, x1, v = jnp.split(dwconv1d(p, lp['hy_conv']), 3, axis=-1)
    z = v * x1
    k2 = hyena_filter(l, lp['hy_w1'], lp['hy_b1'], lp['hy_freq'], lp['hy_w2'], lp['hy_b2'], lp['hy_w3'])
    y = (fft_long_conv(z, k2) + z * lp['hy_bias']) * x0
    gw = HYENA_WIDTH // HYENA_GROUPS
    y = rmsnorm(y.reshape(b, l, HYENA_GROUPS, gw), lp['hy_out_g'].reshape(HYENA_GROUPS, gw))
    return y.reshape(b, l, HYENA_WIDTH)

def to_heads(t, d):
    b, l, _ = t.shape
    return t.reshape(b, l, GLA_HEADS, d).transpose(0, 2, 1, 3)

def _flip(t):
    return jnp.flip(t, axis=2)

def gla_log_gate(r, w, bias):
    return jax.nn.log_sigmoid((r @ w + bias).astype(jnp.float32)) / GLA_GATE_TAU

def gla_chunk_stats(k, v, log_a):
    f32 = jnp.float32
    b, h, l, _ = k.shape
    n = l // GLA_CHUNK
    kc = k.astype(f32).reshape(b, h, n, GLA_CHUNK, GLA_DK)
    vc = v.astype(f32).reshape(b, h, n, GLA_CHUNK, GLA_DV)
    cum = jnp.cumsum(log_a.reshape(b, h, n, GLA_CHUNK, GLA_DK), axis=3)
    last = cum[:, :, :, -1:, :]
    u = jnp.einsum('bhncd,bhnce->bhnde', kc * jnp.exp(last - cum), vc)
    decay = jnp.exp(last[:, :, :, 0, :])
    return kc, vc, cum, u, decay

def gla_state_scan(u, decay, s0, keep_prev):
    def step(s, inp):
        dec, du = inp
        return dec[..., None] * s + du, (s if keep_prev else None)
    return lax.scan(step, s0, (jnp.moveaxis(decay, 2, 0), jnp.moveaxis(u, 2, 0)))

def gla_scan(q, k, v, log_a, s0, strict):
    b, h, l, _ = q.shape
    kc, vc, cum, u, decay = gla_chunk_stats(k, v, log_a)
    s_fin, s_prev = gla_state_scan(u, decay, s0, True)
    qc = (q.astype(jnp.float32) * GLA_DK ** -0.5).reshape(b, h, -1, GLA_CHUNK, GLA_DK)
    qe = qc * jnp.exp(cum)
    scores = jnp.einsum('bhnid,bhnjd->bhnij', qe, kc * jnp.exp(-cum))
    mask = jnp.tril(jnp.ones((GLA_CHUNK, GLA_CHUNK), dtype=bool), k=-1 if strict else 0)
    scores = jnp.where(mask, scores, 0.0)
    out = (jnp.einsum('bhnij,bhnje->bhnie', scores, vc)
           + jnp.einsum('bhnid,bhnde->bhnie', qe, jnp.moveaxis(s_prev, 0, 2)))
    return out.reshape(b, h, l, GLA_DV), s_fin

def gla_final_state(k, v, log_a, s0):
    _, _, _, u, decay = gla_chunk_stats(k, v, log_a)
    s_fin, _ = gla_state_scan(u, decay, s0, False)
    return s_fin

def gla_state_inputs(pg, lp):
    k = to_heads(pg[..., :GLA_QK], GLA_DK)
    v = to_heads(pg[..., GLA_QK:GLA_QK + GLA_V], GLA_DV)
    r_f = pg[..., GLA_QK + GLA_V:GLA_QK + GLA_V + GLA_RANK]
    r_b = pg[..., GLA_QK + GLA_V + GLA_RANK:GLA_STATE_COLS]
    la_f = to_heads(gla_log_gate(r_f, lp['gla_wg_f'], lp['gla_bg_f']), GLA_DK)
    la_b = to_heads(gla_log_gate(r_b, lp['gla_wg_b'], lp['gla_bg_b']), GLA_DK)
    return k, v, la_f, la_b

def gla_context_states(pg, lp):
    k, v, la_f, la_b = gla_state_inputs(pg, lp)
    s0 = jnp.zeros((k.shape[0], GLA_HEADS, GLA_DK, GLA_DV), jnp.float32)
    return gla_final_state(k, v, la_f, s0), gla_final_state(_flip(k), _flip(v), _flip(la_b), s0)

def gla_mixer(pg, lp, s0_f, s0_b):
    k, v, la_f, la_b = gla_state_inputs(pg, lp)
    q = to_heads(pg[..., GLA_STATE_COLS:GLA_STATE_COLS + GLA_QK], GLA_DK)
    g = pg[..., GLA_STATE_COLS + GLA_QK:]
    o_f, s_f = gla_scan(q, k, v, la_f, s0_f, False)
    o_b, s_b = gla_scan(_flip(q), _flip(k), _flip(v), _flip(la_b), s0_b, True)
    o = rmsnorm(o_f + _flip(o_b), lp['gla_out_g'])
    b, _, l, _ = o.shape
    o = o.transpose(0, 2, 1, 3).reshape(b, l, GLA_V).astype(pg.dtype)
    return o * jax.nn.silu(g), s_f, s_b

def mixing_block(h, lp, s0_f, s0_b):
    p = h @ lp['w_in']
    hy = hyena_mixer(p[..., :HYENA_PROJ], lp)
    o, s_f, s_b = gla_mixer(p[..., HYENA_PROJ:], lp, s0_f, s0_b)
    return jnp.concatenate([hy, o], axis=-1) @ lp['w_out'], s_f, s_b

def conv_ffn(h, lp, rows, cols):
    a, u = jnp.split(h @ lp['ffn_w_up'], 2, axis=-1)
    a = dwconv2d(a, lp['ffn_conv'], rows, cols)
    return (jax.nn.silu(a) * u) @ lp['ffn_w_down']

def trunk_layer(x, ctx_x, c, c_ctx, lp, rows, last):
    sa, sca, ga, sf, scf, gf = [m[:, None, :] for m in adaln_params(c, lp['w_mod'], lp['b_mod'])]
    csa, csca, cga, csf, cscf, cgf = adaln_params(c_ctx, lp['w_mod'], lp['b_mod'])
    hc = modulate(rmsnorm(ctx_x, lp['g_attn']), csa, csca)
    if last:
        pgc = hc @ lp['w_in'][:, HYENA_PROJ:HYENA_PROJ + GLA_STATE_COLS]
        s_f, s_b = gla_context_states(pgc, lp)
    else:
        s0 = jnp.zeros((ctx_x.shape[0], GLA_HEADS, GLA_DK, GLA_DV), jnp.float32)
        mix_c, s_f, s_b = mixing_block(hc, lp, s0, s0)
        ctx_x = ctx_x + cga * mix_c
        ctx_x = ctx_x + cgf * conv_ffn(modulate(rmsnorm(ctx_x, lp['g_ffn']), csf, cscf), lp, 1, ctx_x.shape[1])
    h = modulate(rmsnorm(x, lp['g_attn']), sa, sca)
    mix, _, _ = mixing_block(h, lp, s_f, s_b)
    x = x + ga * mix
    x = x + gf * conv_ffn(modulate(rmsnorm(x, lp['g_ffn']), sf, scf), lp, rows, GRID_W)
    return x, ctx_x

def setup_inputs(seed: int = 0) -> dict:
    key = jax.random.key(seed)
    ks = jax.random.split(key, 28)

    def nrm(k, shape, scale):
        return jax.random.normal(k, shape, jnp.float32) * scale

    d = D_MODEL
    return {
        'x': nrm(ks[0], (BATCH, SEQ, d), 1.0),
        'c': nrm(ks[1], (BATCH, d), 1.0),
        'ctx': nrm(ks[2], (BATCH, CTX_LEN, d), 1.0),
        'c_ctx': nrm(ks[3], (d,), 1.0),
        'w_mod': nrm(ks[4], (DEPTH, d, 6 * d), 0.5 * d ** -0.5),
        'b_mod': nrm(ks[5], (DEPTH, 6 * d), 0.02),
        'g_attn': 1.0 + nrm(ks[6], (DEPTH, d), 0.02),
        'w_in': nrm(ks[7], (DEPTH, d, IN_WIDTH), d ** -0.5),
        'hy_conv': nrm(ks[8], (DEPTH, 3, HYENA_PROJ), 3 ** -0.5),
        'hy_w1': nrm(ks[9], (DEPTH, FILTER_EMB, FILTER_HIDDEN), FILTER_EMB ** -0.5),
        'hy_b1': nrm(ks[10], (DEPTH, FILTER_HIDDEN), 0.1),
        'hy_freq': 1.0 + nrm(ks[11], (DEPTH, FILTER_HIDDEN), 0.02),
        'hy_w2': nrm(ks[12], (DEPTH, FILTER_HIDDEN, FILTER_HIDDEN), FILTER_HIDDEN ** -0.5),
        'hy_b2': nrm(ks[13], (DEPTH, FILTER_HIDDEN), 0.1),
        'hy_w3': nrm(ks[14], (DEPTH, FILTER_HIDDEN, 2 * HYENA_WIDTH), FILTER_HIDDEN ** -0.5),
        'hy_bias': nrm(ks[15], (DEPTH, HYENA_WIDTH), 0.5),
        'hy_out_g': 1.0 + nrm(ks[16], (DEPTH, HYENA_WIDTH), 0.02),
        'gla_wg_f': nrm(ks[17], (DEPTH, GLA_RANK, GLA_QK), GLA_RANK ** -0.5),
        'gla_bg_f': nrm(ks[18], (DEPTH, GLA_QK), 0.1),
        'gla_wg_b': nrm(ks[19], (DEPTH, GLA_RANK, GLA_QK), GLA_RANK ** -0.5),
        'gla_bg_b': nrm(ks[20], (DEPTH, GLA_QK), 0.1),
        'gla_out_g': 1.0 + nrm(ks[21], (DEPTH, GLA_DV), 0.02),
        'w_out': nrm(ks[22], (DEPTH, MIX_WIDTH, d), MIX_WIDTH ** -0.5),
        'g_ffn': 1.0 + nrm(ks[23], (DEPTH, d), 0.02),
        'ffn_w_up': nrm(ks[24], (DEPTH, d, 2 * D_FF), d ** -0.5),
        'ffn_conv': nrm(ks[25], (DEPTH, 3, 3, D_FF), 9 ** -0.5),
        'ffn_w_down': nrm(ks[26], (DEPTH, D_FF, d), D_FF ** -0.5),
        'g_final': 1.0 + nrm(ks[27], (d,), 0.02),
    }

def reference(x, c, ctx, c_ctx, w_mod, b_mod, g_attn, w_in, hy_conv, hy_w1, hy_b1, hy_freq, hy_w2, hy_b2, hy_w3,
              hy_bias, hy_out_g, gla_wg_f, gla_bg_f, gla_wg_b, gla_bg_b, gla_out_g, w_out, g_ffn, ffn_w_up,
              ffn_conv, ffn_w_down, g_final):
    rows = x.shape[1] // GRID_W
    ctx_x = ctx
    for l in range(DEPTH):
        lp = {
            'w_mod': w_mod[l], 'b_mod': b_mod[l], 'g_attn': g_attn[l], 'w_in': w_in[l],
            'hy_conv': hy_conv[l], 'hy_w1': hy_w1[l], 'hy_b1': hy_b1[l], 'hy_freq': hy_freq[l],
            'hy_w2': hy_w2[l], 'hy_b2': hy_b2[l], 'hy_w3': hy_w3[l], 'hy_bias': hy_bias[l],
            'hy_out_g': hy_out_g[l], 'gla_wg_f': gla_wg_f[l], 'gla_bg_f': gla_bg_f[l],
            'gla_wg_b': gla_wg_b[l], 'gla_bg_b': gla_bg_b[l], 'gla_out_g': gla_out_g[l],
            'w_out': w_out[l], 'g_ffn': g_ffn[l], 'ffn_w_up': ffn_w_up[l], 'ffn_conv': ffn_conv[l],
            'ffn_w_down': ffn_w_down[l],
        }
        x, ctx_x = trunk_layer(x, ctx_x, c, c_ctx, lp, rows, l == DEPTH - 1)
    return rmsnorm(x, g_final)


_drawn_inputs = setup_inputs


def setup_inputs(seed=0):
    import zlib

    import numpy as np

    out = dict(_drawn_inputs(seed))
    spreads = {}
    factors = {'c_ctx': 3.357,
     'g_attn': 5.981,
     'hy_freq': 8.0,
     'hy_out_g': 8.0,
     'gla_wg_f': 3.255,
     'gla_bg_f': 8.0,
     'gla_wg_b': 2.834,
     'gla_bg_b': 8.0,
     'gla_out_g': 8.0,
     'g_ffn': 8.0,
     'g_final': 2.827}
    for name, (base, spread) in spreads.items():
        noise = np.random.default_rng([zlib.crc32(name.encode()), seed]).standard_normal(out[name].shape)
        drawn = base * np.exp(spread * noise) if base else spread * noise
        out[name] = jnp.asarray(drawn.astype(out[name].dtype))
    for name, factor in factors.items():
        out[name] = (out[name] * factor).astype(out[name].dtype)
    return out
```

```python
from contextlib import ExitStack

import numpy as np

import concourse.bass as bass
from concourse import mybir

ALU = mybir.AluOpType
ACT = mybir.ActivationFunctionType
AXX = mybir.AxisListType.X
F32 = mybir.dt.float32
F32R = mybir.dt.float32r
I32 = mybir.dt.int32

P = 128
D = 2048
T = 256
KT = D // P
HYW = 1024
HEADS, DK, DV, CH = 8, 64, 128, 64
RANK = 16
FF = 5632
FT = FF // P
EPS = 1e-6
GRID_W = 64
NB, BANDS, HID = 33, 16, 64

C_X0, C_X1, C_V = 0, HYW, 2 * HYW
C_K = 3 * HYW
C_GV = C_K + HEADS * DK
C_R = C_GV + HEADS * DV
C_Q = C_R + 2 * RANK
C_G = C_Q + HEADS * DK

HY = []
for half in range(2):
    order = (C_V, C_X1, C_X0) if half == 0 else (C_X1, C_V, C_X0)
    for col in order:
        for j in range(2):
            HY.append((half, col, j))
G_R, G_Q, G_KV, G_G = 12, 13, 15, 18
NGRP = 22

QA, QB = 0, 16
def quad_of(G):
    if G < G_KV:
        return QB + G
    if G < G_G:
        return QB + G_KV + 2 * (G - G_KV)
    return QB + G_KV + 6 + (G - G_G)
QC = quad_of(NGRP - 1) + 1
QD = QC + 8
QE = QD + 2 * (FT // 2)
QEND = QE + 22
NUP = FT // 2

V_C, V_CC, V_GA, V_GF, V_HB, V_HG, V_GG, V_FR, V_B1, V_B2 = 0, 16, 32, 48, 64, 72, 80, 81, 82, 83
V_BM, V_HC, V_FC = 84, 180, 252
NV = V_FC + 9 * FT

(K_ID, K_MEAN, K_ONE, K_TF, K_TB, K_SF, K_SB, K_SC, K_PC, K_AL) = range(10)


def subs_of(G):
    return 8 if G_KV <= G < G_G else 4


def mod_units(G, s):
    if G < G_R:
        return s % 2
    if G == G_R:
        return 0
    return 2 if G_KV <= G < G_G else 1


class Own:

    def __init__(self, eng, sem, base=0):
        self.eng, self.sem, self.n, self.base = eng, sem, 0, base

    def __call__(self, ins):
        ins.then_inc(self.sem, 1)
        self.n += 1
        return ins

    def wait(self, back=0):
        self.eng.wait_ge(self.sem, self.base + self.n - back)


def build(nc, a, out):
    with ExitStack() as ctx:
        BASE = 16512

        def at(name, kb, shape, dt=F32):
            return nc.alloc_sbuf_tensor_at(name, shape, dt, offset=BASE + int(kb * 1024))

        raw = at("raw", 0, [P, 4, 1024])
        hi = at("hi", 16, [P, 4, 1024], F32R)
        lo = at("lo", 32, [P, 4, 1024], F32R)
        hx_hi = at("hx_hi", 48, [P, KT, T], F32R)
        hx_lo = at("hx_lo", 64, [P, KT, T], F32R)
        hc_hi = at("hc_hi", 80, [P, KT, T], F32R)
        hc_lo = at("hc_lo", 96, [P, KT, T], F32R)
        mraw = at("mraw", 112, [P, 2, 1024])
        acc = at("acc", 120, [P, 2, 1024])
        vec = at("vec", 128, [P, NV])
        mcol = at("mcol", 130.75, [P, 2, 32])
        gx = at("gx", 131, [P, 2, 16])
        m2 = at("m2", 131.25, [P, 32])
        g2 = at("g2", 131.5, [P, 16])
        sc = at("sc", 131.625, [P, 2, 16])
        ss = at("ss", 131.75, [P, 8])
        rs = at("rs", 131.875, [P, 4])
        ss3 = at("ss3", 132, [P, 8])
        eps = at("eps", 132.125, [P, 1])
        con = at("con", 132.25, [P, 10, P])
        mask = at("mask", 137.25, [P, 2, CH], I32)
        sel = at("sel", 137.75, [4, 2])
        xtok = at("xtok", 48, [P, 2, D])
        ctok = at("ctok", 64, [P, 2, D])
        cvec = at("cvec", 80, [P, KT, P], F32R)
        w3 = at("w3", 88, [HID, 2 * HYW])
        diag = at("diag", 88, [P, 4, P])
        decay = at("decay", 96, [P, 2, HYW])
        pack = at("pack", 104, [P, 7, P])
        fwd_a = at("fwd_a", 108, [P, 2, 512])
        taps = at("taps", 112, [P, 2, 2 * HYW])
        xn = at("xn", 138, [P, KT, T])
        cn = at("cn", 154, [P, KT, T])
        junk = at("junk", 138, [P, D])
        hsum = at("hsum", 170, [P, 2, HYW])
        hdif = at("hdif", 178, [P, 2, HYW])
        rows4 = at("rows4", 186, [4, 2, 512])
        zf = at("zf", 190, [NB, T])
        w1 = at("w1", 191, [NB, HID])
        w2 = at("w2", 191.5, [HID, HID])
        sa = at("sa", 192, [HID, T])
        sk = at("sk", 193, [HID, T])
        sr = at("sr", 194, [HID, T])
        h1 = at("h1", 195, [HID, T])
        h2 = at("h2", 196, [HID, T])
        fwd = at("fwd", 138, [P, 2, 512])
        inv = at("inv", 142, [P, 4, T])
        bv = at("bv", 146, [P, 4, T])
        bx1 = at("bx1", 150, [P, 4, T])
        bx0 = at("bx0", 154, [P, 4, T])
        zt = at("zt", 158, [P, 2, 512])
        yf = at("yf", 162, [P, 4, 512])
        sq = at("sq", 162, [P, 4, T])
        rt = at("rt", 166, [P, 4, T])
        tt = at("tt", 170, [P, 2, 512])
        hf = at("hf", 170, [P, 4, T])
        hm_hi = at("hm_hi", 174, [P, 8, T], F32R)
        hm_lo = at("hm_lo", 182, [P, 8, T], F32R)
        kre = at("kre", 190, [P, 2, HYW])
        kim = at("kim", 198, [P, 2, HYW])
        ktok = at("ktok", 190, [P, 4, 512])
        vtok = at("vtok", 138, [P, 4, HEADS * DV])
        la = at("la", 154, [P, 2, 4, 512])
        qt = at("qt", 170, [P, 4, T])
        rT = at("rT", 198, [NB, 512])
        wg = at("wg", 200, [NB, 2, 512])
        ea = at("ea", 204, [P, 512])
        ep = at("ep", 198, [P, 2, T])
        ke = at("ke", 200, [P, 2, T])
        kd = at("kd", 202, [P, 2, 2, P])
        kc = at("kc", 204, [P, 2, 2, P])
        gm_hi = at("gm_hi", 80, [P, 8, T], F32R)
        gm_lo = at("gm_lo", 88, [P, 8, T], F32R)
        sg = at("sg", 96, [P, 8, T])
        st = at("st", 104, [P, 2, 4, P])
        qe = at("qe", 108, [P, 2, T])
        scm = at("scm", 110, [P, 2, 2, P])
        gsq = at("gsq", 204, [P, 2, T])
        grt = at("grt", 200, [P, 2, T])
        gt = at("gt", 202, [P, 2, T])
        xm = at("xm", 138, [P, 2, D])
        gab = at("gab", 154, [P, D])
        wt = at("wt", 162, [P, 2, 512])
        dg = at("dg", 166, [P, 2, P])
        h2f = at("h2f", 167, [P, 2, 2, T])
        sqj = at("sqj", 198, [P, 512])
        act_hi = at("act_hi", 154, [P, FT, T], F32R)
        act_lo = at("act_lo", 80, [P, FT, T], F32R)
        ap = at("ap", 198, [P, 2, 4, 66])
        cv = at("cv", 200.25, [P, 2, T])
        a32 = at("a32", 202.25, [P, 2, T])
        cwi = at("cwi", 204.25, [P, 9, 2])
        mraw2 = at("mraw2", 48, [P, 2, 1024])
        acc2 = at("acc2", 56, [P, 2, 1024])
        gfb = at("gfb", 64, [P, D])
        gfin = at("gfin", 72, [P, D])
        dr = at("dr", 198, [P, 2, 2, 512])
        ft_ = at("ft_", 124, [P, 2, 512])

        ps = ctx.enter_context(nc.psum_tensor("ps", [P, 8, 512], F32))

        names = """packed consts_in cload xload ctxload fload wload3 tables raw0 raw1 raw2 raw3 hi_ready lo_dve lo_pool pe_done
            mod_in0 mod_in1 mod_used act_own dve_own pool_own
            vt_ps vt_sb sc_done cv_hi cv_zero cv_ready rows_ps rows_sb col_ps
            sq_done rstd_done diag_ready xn_ps xn_act xn_dve
            f1_ps f1_arg f1_sb f2_ps f2_arg f2_sb h3_ps h3_sb row0 sd_done kf_ps kf_sb
            gx_ready hx_hi_ready hx_ready hc_hi_ready hc_ready grp_ps mid_tap hy_evac z_done zt_ps zt_sb dft_ps cplx y_ps y2_done
            y3_done hsq_done hms_ps hrt_done hy_f32 hy_hi hy_mix r_evac q_evac kv_act kv_dve g_evac red_ps red_sb
            wg_zero wg_in rT_ready rT_one la_ps la_exp la_done cum_ps exps pairs_in kdc u_ps sc_set states o_ps gsq_done gms_ps grt_done g_f32 g_prod g_hi g_mix scm_zero
            x_again ga_bias ga_ps ga_ready wo_ps wo_evac xm_done ssm rstd2 dg2 xt_ps h2_f32 h2_hi h2_ready
            ap_zero cw_now a_evac conv_done silu_done act_f32 act_h act_ready
            gfin_in gf_bias gf_ps gf_ready dn_ps dn_evac dn_sum ssf rstd3 rinv rsum dn_mul xg epsok fin0 fin1 out_done""".split()
        S = {n: ctx.enter_context(nc.semaphore(n)) for n in names}
        RAW = [S[f"raw{i}"] for i in range(4)]
        MOD = [S["mod_in0"], S["mod_in1"]]

        w_mod, w_in, w_out = a["w_mod"][0], a["w_in"][0], a["w_out"][0]
        w_up, w_down, b_mod = a["ffn_w_up"][0], a["ffn_w_down"][0], a["b_mod"][0]

        def piece(w, k0, kn, c0, cn):
            cols = slice(c0, c0 + cn) if isinstance(c0, int) else bass.ds(c0, cn)
            return w[k0 * P:(k0 + kn) * P, cols].rearrange("(t p) c -> p t c", p=P)

        def ident(n=P):
            return con[0:n, K_ID, 0:n]

        def u_slot(d, c):
            return (5, {(0, 0): 0, (0, 2): 1, (1, 2): 2}[d, c]) if c % 2 == 0 else (6, {(0, 1): 0, (1, 1): 1, (1, 3): 2}[d, c])

        block = ctx.enter_context(nc.Block())

        def load_sub(sp, q, l, src, kn, cn):
            r, b = l % 4, q + l // 4
            if not (isinstance(b, int) and b == 0):
                if r < 3:
                    sp.wait_ge(S["lo_dve"], b * 3 - 2 + r)
                else:
                    sp.wait_ge(S["lo_pool"], b)
            sp.dma_start(raw[:, r, 0:kn * cn].rearrange("p (t c) -> p t c", t=kn), src).then_inc(RAW[r], 16)

        def round_sub(act, q, l, n=1024):
            r, b = l % 4, q + l // 4
            act.wait_ge(RAW[r], (b + 1) * 16)
            if not (isinstance(b, int) and b == 0):
                act.wait_ge(S["pe_done"], b * 4 - 3 + r)
            act.activation(hi[:, r, 0:n], raw[:, r, 0:n], ACT.Copy).then_inc(S["hi_ready"], 1)

        def rest_sub(eng, q, l, n=1024):
            r, b = l % 4, q + l // 4
            eng.wait_ge(S["hi_ready"], b * 4 + r + 1)
            eng.tensor_tensor(lo[:, r, 0:n], raw[:, r, 0:n], hi[:, r, 0:n].bitcast(F32), ALU.subtract)\
                .then_inc(S["lo_dve" if r < 3 else "lo_pool"], 1)

        def hi_in(pe, q, l):
            pe.wait_ge(S["hi_ready"], (q + l // 4) * 4 + l % 4 + 1)

        def lo_in(pe, q, l):
            r, b = l % 4, q + l // 4
            if r < 3:
                pe.wait_ge(S["lo_dve"], b * 3 + r + 1)
            else:
                pe.wait_ge(S["lo_pool"], b + 1)

        def mod_chunk(m):
            return (3 * D, 3 * D + 1024, 4 * D, 4 * D + 1024, 2 * D, 2 * D + 1024, 5 * D, 5 * D + 1024)[m // 16]

        def mod_at():
            m, where = 0, {}
            for G in range(NGRP):
                for s in range(subs_of(G)):
                    where[G, s] = list(range(m, m + mod_units(G, s)))
                    m += mod_units(G, s)
            assert m == 96, m
            return where

        MODS = mod_at()
        DMODS = {s: [96 + s - 6] for s in range(6, 38)}

        def sub_src(G, s):
            if G < G_R:
                half, col, j = HY[G]
                return piece(w_in, 4 * s, 4, col + 512 * half + 256 * j, 256), 4, 256
            if G == G_R:
                return piece(w_in, 4 * s, 4, C_R, 2 * RANK), 4, 2 * RANK
            if G < G_KV:
                return piece(w_in, 4 * s, 4, C_Q + 256 * (G - G_Q), 256), 4, 256
            if G < G_G:
                return piece(w_in, 2 * s, 2, C_K + 512 * (G - G_KV), 512), 2, 512
            return piece(w_in, 4 * s, 4, C_G + 256 * (G - G_G), 256), 4, 256

        @block.sync
        def _(sp):
            def row(v, n):
                return v.rearrange("(a n) -> a n", n=n)

            sp.dma_start(con[:, :, :], a["con"].rearrange("p (k n) -> p k n", k=10)).then_inc(S["consts_in"], 16)
            for r0, v in ((V_C, a["c"][0]), (V_CC, a["c_ctx"]), (V_GA, a["g_attn"][0]), (V_GF, a["g_ffn"][0]),
                          (V_HB, a["hy_bias"][0]), (V_HG, a["hy_out_g"][0]), (V_GG, a["gla_out_g"][0])):
                n = v.shape[0] // P
                sp.wait_ge(S["row0"], 1)
                sp.dma_start(pack[r0:r0 + n, 0, :], row(v, P)).then_inc(S["packed"], 16)
            for r0, v in ((V_FR, a["hy_freq"]), (V_B1, a["hy_b1"]), (V_B2, a["hy_b2"])):
                sp.dma_start(pack[r0:r0 + 1, 0, 0:HID], v).then_inc(S["packed"], 16)
            sp.dma_start(pack[0:96, 1, :], row(b_mod, P)).then_inc(S["packed"], 16)
            sp.dma_start(pack[0:72, 2, :], a["hy_conv"][0].rearrange("k (a n) -> (k a) n", n=P)).then_inc(S["packed"], 16)
            fc = a["ffn_conv"][0].rearrange("y x (a n) -> (y x a) n", n=P)
            for i in range(4):
                sp.dma_start(pack[0:99, 3 + i, :], fc[99 * i:99 * i + 99, :]).then_inc(S["packed"], 16)
            sp.dma_start(mask[:, :, :], a["mask"].rearrange("p (t c) -> p t c", t=2)).then_inc(S["cload"], 16)
            sp.dma_start(sel[:, :], a["sel"]).then_inc(S["cload"], 16)
            sp.dma_start(zf[:, :], a["zfeat"]).then_inc(S["fload"], 16)
            sp.dma_start(w1[:, :], a["hy_w1"][0]).then_inc(S["fload"], 16)
            sp.dma_start(w2[:, :], a["hy_w2"][0]).then_inc(S["fload"], 16)

            def a_sub(l):
                load_sub(sp, QA, l, piece(w_mod, 2 * (l % 8), 2, 512 * (l // 8), 512), 2, 512)

            for l in range(4):
                a_sub(l)
            sp.dma_start(w3[:, :], a["hy_w3"][0]).then_inc(S["wload3"], 16)
            sp.dma_start(decay[:, :, :], a["decay"].rearrange("p (t c) -> p t c", t=2)).then_inc(S["wload3"], 16)
            for l in range(4, 8):
                a_sub(l)
            sp.dma_start(xtok[:, :, :], a["x"][0].rearrange("(t p) c -> p t c", p=P)).then_inc(S["xload"], 16)
            for l in range(8, 12):
                a_sub(l)
            sp.dma_start(ctok[:, :, :], a["ctx"][0].rearrange("(t p) c -> p t c", p=P)).then_inc(S["ctxload"], 16)
            sp.dma_start(fwd_a[:, :, :], a["fwd"].rearrange("p (t c) -> p t c", t=2)).then_inc(S["wload3"], 16)
            for l in range(12, 64):
                a_sub(l)

            for G in range(NGRP):
                for s in range(subs_of(G)):
                    src, kn, cn = sub_src(G, s)
                    load_sub(sp, quad_of(G), s, src, kn, cn)
                    for m in MODS[G, s]:
                        if m >= 2:
                            sp.wait_ge(S["mod_used"], m - 1)
                        sp.dma_start(mraw[:, m % 2, :], w_mod[(m % 16) * P:(m % 16 + 1) * P,
                                                              mod_chunk(m):mod_chunk(m) + 1024]).then_inc(MOD[m % 2], 16)
                    if (G, s) == (1, 0):
                        sp.wait_ge(S["hx_ready"], KT)
                        sp.dma_start(fwd[:, :, :], a["fwd"].rearrange("p (t c) -> p t c", t=2)).then_inc(S["tables"], 16)
                        sp.dma_start(inv[:, :, :], a["inv"].rearrange("p (t c) -> p t c", t=4)).then_inc(S["tables"], 16)
                    if (G, s) == (G_Q + 1, 3):
                        sp.wait_ge(S["wg_zero"], 1)
                        for d, (w, b) in enumerate((("gla_wg_f", "gla_bg_f"), ("gla_wg_b", "gla_bg_b"))):
                            sp.dma_start(wg[RANK * d:RANK * d + RANK, d, :], a[w][0]).then_inc(S["wg_in"], 16)
                            sp.dma_start(wg[2 * RANK:NB, d, :], a[b]).then_inc(S["wg_in"], 16)

            for l in range(32):
                load_sub(sp, QC, l, piece(w_out, 2 * (l % 8), 2, 512 * (l // 8), 512), 2, 512)
                if l == 5:
                    sp.wait_ge(S["o_ps"], 4)
                    sp.dma_start(xm[:, :, :], a["x"][0].rearrange("(t p) c -> p t c", p=P)).then_inc(S["x_again"], 16)
                    sp.dma_start(gab[:, :], b_mod[2 * D:3 * D].partition_broadcast(P)).then_inc(S["ga_bias"], 16)

            with sp.Fori(0, NUP) as i:
                for s in range(8):
                    load_sub(sp, QD + i * 2, s, piece(w_up, 4 * (s % 4), 4, i * 256 + FF * (s // 4), 256), 4, 256)

            for l in range(88):
                g, s = divmod(l, 22)
                load_sub(sp, QE, l, piece(w_down, 2 * s, 2, 512 * g, 512), 2, 512)
                if l == 5:
                    sp.wait_ge(S["pe_done"], 4 * QE)
                    sp.dma_start(gfb[:, :], b_mod[5 * D:6 * D].partition_broadcast(P)).then_inc(S["gf_bias"], 16)
                    sp.dma_start(gfin[:, :], a["g_final"].partition_broadcast(P)).then_inc(S["gfin_in"], 16)
                for m in DMODS.get(l, []):
                    sp.wait_ge(S["mod_used"], m - 1)
                    sp.dma_start(mraw2[:, m % 2, :], w_mod[(m % 16) * P:(m % 16 + 1) * P,
                                                           mod_chunk(m):mod_chunk(m) + 1024]).then_inc(MOD[m % 2], 16)
            for t in range(2):
                sp.wait_ge(S[f"fin{t}"], 1)
                sp.dma_start(out[0, P * t:P * t + P, :], xm[:, t, :]).then_inc(S["out_done"], 16)
            sp.wait_ge(S["out_done"], 32)

        @block.tensor
        def _(pe):
            def ch_sub(q, s, banks, x_hi, x_lo, operand=None, width=256):
                nt = max(1, width // P)
                m = min(P, width)
                r = s % 4
                if operand is not None:
                    pe.wait_ge(operand, 4 * (s + 1))
                hi_in(pe, q, s)
                h = hi[:, r, 0:4 * width].rearrange("p (t c) -> p t c", t=4)
                l = lo[:, r, 0:4 * width].rearrange("p (t c) -> p t c", t=4)
                for k in range(4):
                    for j in range(nt):
                        w = h[:, k, j * P:j * P + m]
                        o = ps[0:m, banks[j], 0:T]
                        pe.matmul(o, w, x_hi[:, 4 * s + k, :], start=(s == 0 and k == 0), stop=False)
                        pe.matmul(o, w, x_lo[:, 4 * s + k, :], start=False, stop=False)
                lo_in(pe, q, s)
                for k in range(4):
                    for j in range(nt):
                        mm = pe.matmul(ps[0:m, banks[j], 0:T], l[:, k, j * P:j * P + m], x_hi[:, 4 * s + k, :],
                                       start=False, stop=(s == 3 and k == 3))
                mm.then_inc(S["pe_done"], 1)

            def tok_sub(q, l, s, last, tiles):
                r = l % 4
                hi_in(pe, q, l)
                h = hi[:, r, :].rearrange("p (t c) -> p t c", t=2)
                w = lo[:, r, :].rearrange("p (t c) -> p t c", t=2)
                for k in range(2):
                    for b, th, tl in tiles:
                        pe.matmul(ps[:, b, :], th(2 * s + k), h[:, k, :], start=(s == 0 and k == 0), stop=False)
                        pe.matmul(ps[:, b, :], tl(2 * s + k), h[:, k, :], start=False, stop=False)
                lo_in(pe, q, l)
                for k in range(2):
                    for b, th, tl in tiles:
                        mm = pe.matmul(ps[:, b, :], th(2 * s + k), w[:, k, :], start=False, stop=(s == last and k == 1))
                mm.then_inc(S["pe_done"], 1)

            pe.wait_ge(S["consts_in"], 16)
            pe.wait_ge(S["packed"], 16 * 16)
            for i, (n, c0) in enumerate(((84, V_C), (96, V_BM), (72, V_HC))):
                pe.transpose(ps[:, 3, c0:c0 + n], pack[0:n, i, :], ident(n)).then_inc(S["vt_ps"], 1)
            for i in range(4):
                pe.transpose(ps[:, 4, 99 * i:99 * i + 99], pack[0:99, 3 + i, :], ident(99)).then_inc(S["vt_ps"], 1)

            def filter_hidden(w, x, sem, bank):
                pe.matmul(ps[0:HID, bank, 0:T], w, x, start=True, stop=True).then_inc(sem, 1)

            def filter_out(j0):
                for j in range(j0, j0 + 4):
                    if j >= 4:
                        pe.wait_ge(S["h3_sb"], j - 3)
                    t, c = divmod(j, 4)
                    pe.matmul(ps[:, 4 + j % 4, :], h2[:, P * t:P * t + P], w3[:, 512 * c:512 * c + 512],
                              start=True, stop=True).then_inc(S["h3_ps"], 1)

            def spectrum(part):
                src = (hsum, hdif)[part]
                for j in range(4):
                    n = 4 * part + j
                    f, c = divmod(j, 2)
                    if n >= 4:
                        pe.wait_ge(S["kf_sb"], n - 3)
                    else:
                        pe.wait_ge(S["h3_sb"], 8)
                    for t in range(2):
                        mm = pe.matmul(ps[:, 4 + j, :], fwd_a[:, t, 256 * part + P * f:256 * part + P * f + P],
                                       src[:, t, 512 * c:512 * c + 512], start=(t == 0), stop=(t == 1))
                    mm.then_inc(S["kf_ps"], 1)

            def nyquist():
                for c in range(2):
                    pe.wait_ge(S["kf_sb"], 5 + c)
                    for t in range(2):
                        mm = pe.matmul(ps[0:1, 4 + c, :], fwd_a[:, t, 256:257], hsum[:, t, 512 * c:512 * c + 512],
                                       start=(t == 0), stop=(t == 1))
                    mm.then_inc(S["kf_ps"], 1)

            def norm_turn(t):
                if t < 4:
                    pe.wait_ge(S["kf_sb"], 10)
                else:
                    pe.wait_ge(S[("xn_act", "xn_dve")[t % 2]], 2 * ((t - 4) // 2 + 1))
                for j in range(4):
                    src = (xtok, ctok)[j // 2]
                    mm = pe.matmul(ps[:, 4 + t % 4, P * j:P * j + P], src[:, j % 2, P * t:P * t + P], diag[:, j, :],
                                   start=True, stop=True)
                mm.then_inc(S["xn_ps"], 1)

            def rows_to_cols(g):
                pe.wait_ge(S["rows_sb"], g + 1)
                for c in range(4):
                    mm = pe.matmul(ps[:, 2, 2 * (4 * g + c):2 * (4 * g + c) + 2], rows4[:, g % 2, P * c:P * c + P],
                                   sel[:, :], start=True, stop=True)
                mm.then_inc(S["col_ps"], 1)

            pe.wait_ge(S["cload"], 32)
            for g in range(8):
                for s in range(8):
                    l = 8 * g + s
                    if s == 0:
                        if g == 0:
                            pe.wait_ge(S["cv_ready"], 2)
                        if g >= 2:
                            pe.wait_ge(S["rows_sb"], g - 1)
                    hi_in(pe, QA, l)
                    h = hi[:, l % 4, :].rearrange("p (t c) -> p t c", t=2)
                    lw = lo[:, l % 4, :].rearrange("p (t c) -> p t c", t=2)
                    for k in range(2):
                        pe.matmul(ps[:, g % 2, :], cvec[:, 2 * s + k, :], h[:, k, :], start=(s == 0 and k == 0), stop=False)
                    lo_in(pe, QA, l)
                    for k in range(2):
                        mm = pe.matmul(ps[:, g % 2, :], cvec[:, 2 * s + k, :], lw[:, k, :], start=False,
                                       stop=(s == 7 and k == 1))
                    mm.then_inc(S["pe_done"], 1)
                    if g >= 1 and s == 5:
                        rows_to_cols(g - 1)
                    if (g, s) == (0, 3):
                        pe.wait_ge(S["fload"], 48)
                        pe.wait_ge(S["vt_sb"], 2)
                        filter_hidden(w1[:, :], zf[:, :], S["f1_ps"], 5)
                    if (g, s) == (0, 7):
                        pe.wait_ge(S["f1_sb"], 1)
                        filter_hidden(w2[:, :], h1[:, :], S["f2_ps"], 6)
                    if (g, s) == (1, 3):
                        pe.wait_ge(S["f2_sb"], 1)
                        pe.wait_ge(S["wload3"], 48)
                        filter_out(0)
                    if (g, s) == (1, 7):
                        filter_out(4)
                    if (g, s) == (3, 1):
                        pe.wait_ge(S["sd_done"], 1)
                        spectrum(0)
                    if (g, s) == (3, 4):
                        pe.wait_ge(S["sd_done"], 2)
                        spectrum(1)
                    if (g, s) == (3, 7):
                        nyquist()
                    if g in (4, 5) and s % 2:
                        if (g, s) == (4, 1):
                            pe.wait_ge(S["diag_ready"], 4)
                        norm_turn(8 * (g - 4) + s - 1)
                        norm_turn(8 * (g - 4) + s)
            rows_to_cols(7)

            def turn_z(h):
                pe.wait_ge(S["z_done"], h + 1)
                if h == 0:
                    pe.wait_ge(S["xn_act"], KT)
                    pe.wait_ge(S["xn_dve"], KT)
                else:
                    pe.wait_ge(S["y2_done"], 4 * h)
                for t in range(2):
                    for j in range(4):
                        mm = pe.transpose(ps[:, 4 + t, P * j:P * j + P], bv[:, j, P * t:P * t + P], ident())
                    mm.then_inc(S["zt_ps"], 1)

            def dft(h):
                pe.wait_ge(S["zt_sb"], 2 * (h + 1))
                pe.wait_ge(S["tables"], 32)
                if h == 1:
                    pe.wait_ge(S["hrt_done"], 1)
                for f in range(4):
                    for t in range(2):
                        mm = pe.matmul(ps[:, 4 + f, :], fwd[:, t, P * f:P * f + P], zt[:, t, :], start=(t == 0), stop=(t == 1))
                mm.then_inc(S["dft_ps"], 1)

            def dft_back(h):
                pe.wait_ge(S["cplx"], h + 1)
                for j in range(4):
                    for f in range(4):
                        mm = pe.matmul(ps[:, 4 + j // 2, T * (j % 2):T * (j % 2) + T], yf[:, f, P * j:P * j + P],
                                       inv[:, f, :], start=(f == 0), stop=(f == 3))
                mm.then_inc(S["y_ps"], 1)

            def group_mean(h):
                pe.wait_ge(S["hsq_done"], h + 1)
                for j in range(2):
                    mm = pe.matmul(ps[:, 6 + j, :], con[:, K_MEAN, :], sq[:, 2 * j:2 * j + 2, :], start=True, stop=True)
                mm.then_inc(S["hms_ps"], 1)

            def reduce_cols(chunk, bank, c0):
                pe.wait_ge(S["mod_used"], 16 * (chunk + 1))
                for c in range(8):
                    mm = pe.matmul(ps[:, bank, c0 + c:c0 + c + 1], acc[:, chunk % 2, P * c:P * c + P], con[:, K_ONE, 0:1],
                                   start=True, stop=True)
                mm.then_inc(S["red_ps"], 1)

            def gates(j):
                d, t = divmod(j, 4)
                if j == 0:
                    pe.wait_ge(S["rT_ready"], 2)
                    pe.wait_ge(S["rT_one"], 1)
                    pe.wait_ge(S["wg_in"], 64)
                    pe.wait_ge(S["hrt_done"], 2)
                if j >= 3:
                    pe.wait_ge(S["la_done"], j - 2)
                pe.matmul(ps[:, 4 + j % 3, :], rT[:, P * t:P * t + P], wg[:, d, :], start=True, stop=True)\
                    .then_inc(S["la_ps"], 1)

            def pair_sums(p):
                cs = slice(P * p, P * p + P)
                if p == 0:
                    pe.wait_ge(S["la_done"], 8)
                    pe.wait_ge(S["red_sb"], 4)
                    pe.wait_ge(S["kv_act"], 1)
                    pe.wait_ge(S["kv_dve"], 1)
                else:
                    pe.wait_ge(S["g_f32"], p)
                    pe.wait_ge(S["grt_done"], p)
                for d, tri in enumerate((K_TF, K_TB)):
                    for t in range(2):
                        pe.matmul(ps[:, 4, 256 * d + P * t:256 * d + P * t + P], la[:, d, t, cs], con[:, tri, :],
                                  start=True, stop=True)
                for d, tri in enumerate((K_SF, K_SB)):
                    for t in range(2):
                        pe.matmul(ps[:, 5, 256 * d + P * t:256 * d + P * t + P], con[:, tri, :], la[:, d, t, cs],
                                  start=True, stop=True)
                pe.matmul(ps[:, 6, 0:P], con[:, K_SC, :], la[:, 0, 2, cs], start=True, stop=False)
                pe.matmul(ps[:, 6, 0:P], con[:, K_AL, :], la[:, 0, 3, cs], start=False, stop=True)
                pe.matmul(ps[:, 6, P:2 * P], con[:, K_SC, :], la[:, 0, 3, cs], start=True, stop=True)
                pe.matmul(ps[:, 6, 2 * P:3 * P], con[:, K_PC, :], la[:, 1, 2, cs], start=True, stop=True)
                pe.matmul(ps[:, 6, 3 * P:4 * P], con[:, K_PC, :], la[:, 1, 3, cs], start=True, stop=False)
                pe.matmul(ps[:, 6, 3 * P:4 * P], con[:, K_AL, :], la[:, 1, 2, cs], start=False, stop=True)
                for t in range(2):
                    mm = pe.transpose(ps[:, 7, P * t:P * t + P], ktok[:, t, cs], ident())
                mm.then_inc(S["cum_ps"], 1)

            def pair_products(p):
                pe.wait_ge(S["kdc"], 4 * (p + 1))
                pe.wait_ge(S["pairs_in"], 4 * (p + 1))
                if p == 0:
                    pe.wait_ge(S["kv_act"], 3)
                    pe.wait_ge(S["kv_dve"], 3)
                for d in range(2):
                    for hh in range(2):
                        for t in range(2):
                            pe.matmul(ps[64 * hh:64 * hh + 64, 5 + d, 3 * P:4 * P], kc[:, d, t, 64 * hh:64 * hh + 64],
                                      vtok[:, 2 + t, DV * (2 * p + hh):DV * (2 * p + hh) + DV], start=(t == 0), stop=(t == 1))
                for d, c in ((0, 0), (0, 2), (1, 2), (0, 1), (1, 1), (1, 3)):
                    b, slot = u_slot(d, c)
                    r0 = 64 * (c % 2)
                    for hh in range(2):
                        mm = pe.matmul(ps[64 * hh:64 * hh + 64, b, P * slot:P * slot + P],
                                       kd[r0:r0 + 64, d, c // 2, 64 * hh:64 * hh + 64],
                                       vtok[r0:r0 + 64, c // 2, DV * (2 * p + hh):DV * (2 * p + hh) + DV],
                                       start=True, stop=True)
                mm.then_inc(S["u_ps"], 1)
                for hh in range(2):
                    b = 7 if hh == 0 else 4
                    rr = slice(64 * hh, 64 * hh + 64)
                    for t in range(2):
                        for d in range(2):
                            mm = pe.matmul(ps[:, b, P * (2 * t + d):P * (2 * t + d) + P], ke[rr, d, P * t:P * t + P],
                                           qe[rr, d, P * t:P * t + P], start=True, stop=True)
                    mm.then_inc(S["u_ps"], 1)

            def pair_out(p):
                pe.wait_ge(S["sc_set"], 8 * (p + 1))
                pe.wait_ge(S["states"], 8 * (p + 1))
                for hh in range(2):
                    rr = slice(64 * hh, 64 * hh + 64)
                    hcol = slice(DV * (2 * p + hh), DV * (2 * p + hh) + DV)
                    for t in range(2):
                        pe.matmul(ps[:, 5 + hh, P * t:P * t + P], vtok[:, t, hcol], scm[:, hh, t, :], start=True, stop=False)
                        for c in (2 * t, 2 * t + 1):
                            for d in range(2):
                                mm = pe.matmul(ps[:, 5 + hh, CH * c:CH * c + CH], st[rr, d, c, :],
                                               qe[rr, d, CH * c:CH * c + CH], start=False,
                                               stop=(c == 2 * t + 1 and d == 1))
                mm.then_inc(S["o_ps"], 1)

            def pair_mean(p):
                pe.wait_ge(S["gsq_done"], p + 1)
                pe.matmul(ps[:, 7, :], con[:, K_MEAN, :], gsq[:, :, :], start=True, stop=True).then_inc(S["gms_ps"], 1)

            def pair_step(slot):
                p, k = divmod(slot + 1, 5)
                if 0 <= p < 4 and slot > 0:
                    if k == 0:
                        pair_sums(p)
                    if k == 2:
                        pair_products(p)
                    if k == 3:
                        pair_out(p)
                    if k == 4:
                        pair_mean(p)

            for G in range(NGRP):
                q = quad_of(G)
                pair = (2 * (G % 2), 2 * (G % 2) + 1)
                for s in range(subs_of(G)):
                    if s == 0:
                        if G == 0:
                            pe.wait_ge(S["rows_sb"], 8)
                        elif G == 1:
                            pe.wait_ge(S["gx_ready"], 4)
                        elif G <= G_R:
                            pe.wait_ge(S["hy_evac"], 2 * (G - 1))
                        elif G == G_Q:
                            pe.wait_ge(S["hy_evac"], 24)
                        elif G == G_Q + 1:
                            pe.wait_ge(S["rT_ready"], 2)
                        elif G < G_G:
                            if G == G_KV:
                                pe.wait_ge(S["q_evac"], 2)
                            else:
                                pe.wait_ge(S["kv_act"], G - G_KV)
                                pe.wait_ge(S["kv_dve"], G - G_KV)
                        elif G < G_G + 2:
                            pe.wait_ge(S["kv_act"], 3)
                            pe.wait_ge(S["kv_dve"], 3)
                        else:
                            pe.wait_ge(S["g_evac"], G - G_G - 1)
                        if G == 9:
                            reduce_cols(0, pair[0], 256)
                    if G == G_R:
                        pe.wait_ge(S["hc_ready"], KT)
                        hi_in(pe, q, s)
                        h = hi[:, s, 0:128].rearrange("p (t c) -> p t c", t=4)
                        lw = lo[:, s, 0:128].rearrange("p (t c) -> p t c", t=4)
                        for k in range(4):
                            for b, th, tl in ((0, hx_hi, hx_lo), (1, hc_hi, hc_lo)):
                                kk = 4 * s + k
                                first = s == 0 and k == 0
                                pe.matmul(ps[0:32, b, 0:T], h[:, k, :], th[:, kk, :], start=first, stop=False,
                                          )
                                pe.matmul(ps[0:32, b, 0:T], h[:, k, :], tl[:, kk, :], start=False, stop=False)
                        lo_in(pe, q, s)
                        for k in range(4):
                            for b, th in ((0, hx_hi), (1, hc_hi)):
                                mm = pe.matmul(ps[0:32, b, 0:T], lw[:, k, :], th[:, 4 * s + k, :], start=False,
                                               stop=(s == 3 and k == 3))
                        mm.then_inc(S["pe_done"], 1)
                    elif G_KV <= G < G_G:
                        def tile_of(x, t):
                            return lambda k: x[:, k, P * t:P * t + P]
                        tok_sub(q, s, s, 7, [(b, tile_of((hx_hi, hc_hi)[b // 2], b % 2), tile_of((hx_lo, hc_lo)[b // 2], b % 2))
                                          for b in range(4)])
                    else:
                        ch_sub(q, s, pair, hx_hi, hx_lo, operand=S["hx_ready"] if G == 0 else None)
                    for h, at5, at3, ay, am in ((0, (5, 0), (5, 3), (6, 3), (8, 0)), (1, (11, 0), (11, 3), (G_R, 3), (G_Q + 1, 0))):
                        if (G, s) == at5:
                            turn_z(h)
                        if (G, s) == at3:
                            dft(h)
                        if (G, s) == ay:
                            dft_back(h)
                        if (G, s) == am:
                            group_mean(h)
                    if G_KV <= G < G_G and s == 1:
                        if G == G_KV:
                            pe.wait_ge(S["hrt_done"], 2)
                        else:
                            pe.wait_ge(S["red_sb"], 1 + G - G_KV)
                        reduce_cols(1 + G - G_KV, 7, 0)
                    if G == G_KV + 1:
                        gates(s)
                    if (G, s) == (G_KV + 2, 5):
                        pair_sums(0)
                    if G >= G_G:
                        pair_step(4 * (G - G_G) + s)

            for g in range(4):
                for s in range(8):
                    if s == 0:
                        if g < 2:
                            pe.wait_ge(S["g_evac"], 3 + g)
                        else:
                            pe.wait_ge(S["wo_evac"], 2 * (g - 1))
                    if g == 0 and s == 0:
                        pe.wait_ge(S["hy_mix"], 2)
                    if g == 0 and s >= 4:
                        pe.wait_ge(S["g_mix"], s - 3)
                    def mix(x, y, t):
                        return lambda k: (x[:, k, P * t:P * t + P] if k < 8 else y[:, k - 8, P * t:P * t + P])
                    b0 = 2 * (g % 2)
                    tok_sub(QC + 2 * g, s, s, 7, [(b0 + t, mix(hm_hi, gm_hi, t), mix(hm_lo, gm_lo, t)) for t in range(2)])
                    if g == 0:
                        pair_step(16 + s)
                    if (g, s) == (0, 6):
                        pe.wait_ge(S["mod_used"], 96)
                        pe.wait_ge(S["grt_done"], 4)
                        pe.wait_ge(S["g_f32"], 4)
                        for c in range(4):
                            mm = pe.matmul(ps[:, 4 + c, :], con[:, K_ONE, :], acc[:, c // 2, 512 * (c % 2):512 * (c % 2) + 512],
                                           start=True, stop=True)
                        mm.then_inc(S["ga_ps"], 1)
            pe.wait_ge(S["ga_ready"], 1)
            pe.wait_ge(S["dg2"], 2)
            for j in range(8):
                if j >= 4:
                    pe.wait_ge(S["h2_f32"], 2 * (j - 3))
                for i in range(2):
                    for t in range(2):
                        k = 2 * j + i
                        mm = pe.matmul(ps[:, 4 + j % 4, 256 * i + P * t:256 * i + P * t + P], xm[:, t, P * k:P * k + P],
                                       dg[:, t, :], start=True, stop=True)
                mm.then_inc(S["xt_ps"], 1)

            pe.wait_ge(S["wo_evac"], 8)
            pe.wait_ge(S["h2_ready"], 8)
            with pe.Fori(0, NUP) as i:
                for s in range(8):
                    if s == 0:
                        pe.wait_ge(S["a_evac"], i * 2)
                    if s == 4:
                        pe.wait_ge(S["act_f32"], i)
                    g = s // 4
                    r = s % 4
                    q = QD + i * 2
                    hi_in(pe, q, s)
                    h = hi[:, r, :].rearrange("p (t c) -> p t c", t=4)
                    l = lo[:, r, :].rearrange("p (t c) -> p t c", t=4)
                    for k in range(4):
                        for j in range(2):
                            o = ps[:, 2 * g + j, 0:T]
                            pe.matmul(o, h[:, k, j * P:j * P + P], hx_hi[:, 4 * r + k, :], start=(r == 0 and k == 0), stop=False)
                            pe.matmul(o, h[:, k, j * P:j * P + P], hx_lo[:, 4 * r + k, :], start=False, stop=False)
                    lo_in(pe, q, s)
                    for k in range(4):
                        for j in range(2):
                            mm = pe.matmul(ps[:, 2 * g + j, 0:T], l[:, k, j * P:j * P + P], hx_hi[:, 4 * r + k, :],
                                           start=False, stop=(r == 3 and k == 3))
                    mm.then_inc(S["pe_done"], 1)

            def act_of(x, t):
                return lambda k: x[:, k, P * t:P * t + P]

            for g in range(4):
                for s in range(22):
                    if s == 0:
                        if g == 0:
                            pe.wait_ge(S["a_evac"], 2 * NUP)
                            pe.wait_ge(S["act_ready"], NUP - 1)
                        if g == 1:
                            pe.wait_ge(S["act_f32"], NUP)
                        if g >= 2:
                            pe.wait_ge(S["dn_evac"], 2 * (g - 1))
                    if g == 0 and s == 21:
                        pe.wait_ge(S["act_ready"], NUP)
                    b0 = 2 * (g % 2)
                    tok_sub(QE, 22 * g + s, s, 21, [(b0 + t, act_of(act_hi, t), act_of(act_lo, t)) for t in range(2)])
                    if (g, s) == (1, 18):
                        pe.wait_ge(S["mod_used"], 128)
                        for c in range(4):
                            mm = pe.matmul(ps[:, 4 + c, :], con[:, K_ONE, :], acc2[:, c // 2, 512 * (c % 2):512 * (c % 2) + 512],
                                           start=True, stop=True)
                        mm.then_inc(S["gf_ps"], 1)

        PROD = {6: 0, 10: 1, 14: 2, 20: 3}

        @block.scalar
        def _(act):
            def f(o, i, fn, sem, **kw):
                act.activation(o, i, fn, **kw).then_inc(S[sem], 1)

            act.wait_ge(S["vt_sb"], 2)
            f(sc[:, :, :], vec[:, 0:32].rearrange("p (a b) -> p a b", a=2), ACT.Silu, "sc_done")
            act.wait_ge(S["sc_done"], 1)
            act.wait_ge(S["cv_zero"], 1)
            for j in range(2):
                f(cvec[:, :, 2 * j], sc[:, j, :], ACT.Copy, "cv_hi")

            def turn_evac(t):
                act.wait_ge(S["xn_ps"], t + 1)
                f(xn[:, t, :], ps[:, 4 + t % 4, 0:T], ACT.Copy, "xn_act")
                f(cn[:, t, :], ps[:, 4 + t % 4, T:2 * T], ACT.Copy, "xn_act")

            def square_in(j):
                act.wait_ge(S["xload" if j < 2 else "ctxload"], 16)
                if j:
                    act.wait_ge(S["sq_done"], j)
                act.activation(junk[:, :], (xtok, ctok)[j // 2][:, j % 2, :], ACT.Square, accum_out=ss[:, j:j + 1])\
                    .then_inc(S["sq_done"], 1)

            for g in range(8):
                for s in range(8):
                    round_sub(act, QA, 8 * g + s)
                    if (g, s) == (0, 5):
                        act.wait_ge(S["f1_arg"], 1)
                        f(h1[:, :], sr[:, :], ACT.Sin, "f1_sb")
                    if (g, s) == (1, 1):
                        act.wait_ge(S["f2_arg"], 1)
                        f(h2[:, :], sr[:, :], ACT.Sin, "f2_sb")
                    if g == 1 and s in (4, 6):
                        square_in((s - 4) // 2)
                    if g == 2 and s in (0, 3):
                        square_in(2 + s // 3)
                    if (g, s) == (2, 5):
                        act.wait_ge(S["sq_done"], 4)
                        act.wait_ge(S["epsok"], 1)
                        f(rs[:, 0:4], ss[:, 0:4], ACT.Sqrt, "rstd_done", scale=1.0 / D, bias=eps[:, 0:1])
                    for part, at_ in ((0, (3, 3)), (1, (3, 6))):
                        if (g, s) == at_:
                            for j in range(4):
                                act.wait_ge(S["kf_ps"], 4 * part + j + 1)
                                if part == 0 and j == 0:
                                    act.wait_ge(S["h3_ps"], 8)
                                f((kre, kim)[part][:, j // 2, 512 * (j % 2):512 * (j % 2) + 512], ps[:, 4 + j, :],
                                  ACT.Copy, "kf_sb")
                    if (g, s) == (4, 0):
                        for c in range(2):
                            act.wait_ge(S["kf_ps"], 9 + c)
                            act.wait_ge(S["kf_sb"], 8)
                            f(kim[0:1, 0, 512 * c:512 * c + 512], ps[0:1, 4 + c, :], ACT.Copy, "kf_sb")
                    if (g, s) in [(4, 3), (4, 5), (4, 7), (5, 1), (5, 3), (5, 5), (5, 7), (6, 0)]:
                        turn_evac(2 * [(4, 3), (4, 5), (4, 7), (5, 1), (5, 3), (5, 5), (5, 7), (6, 0)].index((g, s)))

            def operand_hi(t, src, dst, j, sem):
                f(dst[:, t, :], src[:, t, :], ACT.Identity, sem, scale=gx[:, j, t:t + 1], bias=mcol[:, j, t:t + 1])

            def hy_mid(G):
                half, col, jg = HY[G]
                dst = {C_V: bv, C_X1: bx1, C_X0: bx0}[col]
                if half == 0:
                    act.wait_ge(S["hx_ready"], KT)
                    if col == C_X0:
                        act.wait_ge(S["hc_ready"], KT)
                elif col == C_X1:
                    act.wait_ge(S["z_done"], 1)
                elif col == C_V:
                    act.wait_ge(S["hy_mix"], 1)
                else:
                    act.wait_ge(S["y3_done"], 1)
                act.wait_ge(S["pe_done"], 4 * (quad_of(G) + 1))
                for jj in range(2):
                    tile = col // P + 4 * half + 2 * jg + jj
                    f(dst[:, 2 * jg + jj, :], ps[:, 2 * (G % 2) + jj, 0:T], ACT.Copy, "mid_tap",
                      scale=vec[:, V_HC + 24 + tile:V_HC + 25 + tile])

            def hyena(h, step):
                if step == 0:
                    for t in range(2):
                        act.wait_ge(S["zt_ps"], 2 * h + t + 1)
                        if h == 1:
                            act.wait_ge(S["dft_ps"], 1)
                        f(zt[:, t, :], ps[:, 4 + t, :], ACT.Copy, "zt_sb")
                if step == 1:
                    act.wait_ge(S["y3_done"], h + 1)
                    f(sq[:, :, :], bv[:, :, :], ACT.Square, "hsq_done")
                if step == 2:
                    act.wait_ge(S["hms_ps"], h + 1)
                    f(rt[:, :, :], ps[:, 6:8, :].rearrange("p b (j c) -> p (b j) c", j=2), ACT.Sqrt, "hrt_done",
                      bias=eps[:, 0:1])
                if step == 3:
                    act.wait_ge(S["hy_f32"], 4 * (h + 1))
                    f(hm_hi[:, 4 * h:4 * h + 4, :], bv[:, :, :], ACT.Copy, "hy_hi")

            def kv_evac(G):
                act.wait_ge(S["pe_done"], 4 * quad_of(G) + 8)
                if G == G_KV:
                    act.wait_ge(S["cplx"], 2)
                else:
                    act.wait_ge(S["hy_mix"], 2)
                for b in range(2):
                    dst = ktok[:, b, :] if G == G_KV else vtok[:, b, 512 * (G - G_KV - 1):512 * (G - G_KV)]
                    ins = act.activation(dst, ps[:, b, :], ACT.Copy)
                ins.then_inc(S["kv_act"], 1)

            def softplus(j):
                act.wait_ge(S["la_ps"], j + 1)
                if j:
                    act.wait_ge(S["la_done"], j)
                f(ea[:, :], ps[:, 4 + j % 3, :], ACT.Abs, "act_own")
                act.wait_ge(S["act_own"], 2 * j + 1)
                f(ea[:, :], ea[:, :], ACT.Exp, "act_own", scale=-1.0)
                act.wait_ge(S["act_own"], 2 * j + 2)
                f(ea[:, :], ea[:, :], ACT.Ln, "la_exp", bias=1.0)

            def gla(slot):
                p, k = divmod(slot, 5)
                if k == 0 and p < 4:
                    act.wait_ge(S["cum_ps"], p + 1)
                    flat = "p a b -> p (a b)"
                    f(ep[:, :, :].rearrange(flat), ps[:, 4, :], ACT.Exp, "exps")
                    f(ke[:, :, :].rearrange(flat), ps[:, 4, :], ACT.Exp, "exps", scale=-1.0)
                    f(kd[:, :, :, :].rearrange("p a b c -> p (a b c)"), ps[:, 5, :], ACT.Exp, "exps")
                    f(kc[:, :, :, :].rearrange("p a b c -> p (a b c)"), ps[:, 6, :], ACT.Exp, "exps")
                if k == 3 and p < 4:
                    act.wait_ge(S["o_ps"], p + 1)
                    f(gsq[:, :, :], ps[:, 5:7, 0:T], ACT.Square, "gsq_done")
                if k == 4 and p < 4:
                    act.wait_ge(S["gms_ps"], p + 1)
                    f(grt[:, :, :].rearrange("p a b -> p (a b)"), ps[:, 7, :], ACT.Sqrt, "grt_done", bias=eps[:, 0:1])
                if slot % 4 == 2 and slot >= 6 and (slot - 6) // 4 < 4:
                    g = (slot - 6) // 4
                    act.wait_ge(S["pe_done"], 4 * (quad_of(G_G + g) + 1))
                    if g == 3:
                        act.wait_ge(S["g_mix"], 1)
                    z = (2 * g + 2) % 8
                    f(sg[:, z:z + 2, :], ps[:, 2 * (g % 2):2 * (g % 2) + 2, 0:T], ACT.Silu, "g_evac")
                if slot - 1 in PROD:
                    p = PROD[slot - 1]
                    act.wait_ge(S["g_prod"], p + 1)
                    f(gm_hi[:, 2 * p:2 * p + 2, :], sg[:, 2 * p:2 * p + 2, :], ACT.Copy, "g_hi")

            HYS = {(5, 2): (0, 0), (7, 3): (0, 1), (8, 1): (0, 2), (8, 3): (0, 3),
                   (11, 2): (1, 0), (G_Q + 1, 0): (1, 1), (G_Q + 1, 1): (1, 2), (G_Q + 1, 3): (1, 3)}
            act.wait_ge(S["gx_ready"], 4)
            act.wait_ge(S["xn_dve"], KT)
            act.wait_ge(S["xn_act"], KT)
            for G in range(NGRP):
                for s in range(subs_of(G)):
                    if G == 0:
                        for t in range(4 * s, 4 * s + 4):
                            operand_hi(t, xn, hx_hi, 0, "hx_hi_ready")
                    round_sub(act, quad_of(G), s, 128 if G == G_R else 1024)
                    if G < 4:
                        operand_hi(4 * G + s, cn, hc_hi, 1, "hc_hi_ready")
                    if 1 <= G <= G_R and s == 2:
                        hy_mid(G - 1)
                    if (G, s) in HYS:
                        hyena(*HYS[G, s])
                    if G_KV < G <= G_G and s == 0:
                        kv_evac(G - 1)
                    if G == G_KV + 1 and s >= 1:
                        softplus(s - 1)
                    if (G, s) == (G_KV + 2, 0):
                        softplus(7)
                    if (G, s) == (G_KV + 2, 7):
                        gla(0)
                    if G >= G_G and (G, s) != (G_G, 0):
                        gla(4 * (G - G_G) + s)

            def ssq(g):
                for t in range(2):
                    act.wait_ge(S["xm_done"], 2 * g + t + 1)
                    if g + t:
                        act.wait_ge(S["ssm"], 2 * g + t)
                    act.activation(sqj[:, :], xm[:, t, 512 * g:512 * g + 512], ACT.Square,
                                   accum_out=ss[:, 4 * t + g:4 * t + g + 1]).then_inc(S["ssm"], 1)

            for g in range(4):
                for s in range(8):
                    round_sub(act, QC + 2 * g, s)
                    if g == 0:
                        gla(16 + s)
                    if g >= 1 and s == 3:
                        ssq(g - 1)
            ssq(3)
            act.wait_ge(S["rsum"], 1)
            f(rs[:, 0:2], rs[:, 0:2], ACT.Sqrt, "rstd2", scale=1.0 / D, bias=eps[:, 0:1])
            for j in range(8):
                act.wait_ge(S["h2_f32"], 2 * j + 2)
                f(hx_hi[:, 2 * j:2 * j + 2, :], h2f[:, j % 2, :, :], ACT.Copy, "h2_hi")

            def silu_of(i):
                act.wait_ge(S["conv_done"], i + 1)
                f(cv[:, :, :], cv[:, :, :], ACT.Silu, "silu_done")

            def act_hi_of(i):
                act.wait_ge(S["act_f32"], i + 1)
                f(act_hi[:, bass.ds(i * 2, 2), :], a32[:, :, :], ACT.Copy, "act_h")

            def up_body(i, first):
                q = QD + i * 2
                for s in range(8):
                    if s == 7:
                        act.wait_ge(S["pe_done"], q * 4 + 4)
                        act.wait_ge(S["conv_done"], i)
                        for j in range(2):
                            f(ap[:, j, :, 1:65], ps[:, j, 0:T].rearrange("p (y x) -> p y x", y=4), ACT.Copy, "a_evac")
                    round_sub(act, q, s)
                    if s == 0 and not first:
                        silu_of(i - 1)
                    if s == 3 and not first:
                        act_hi_of(i - 1)

            act.wait_ge(S["ap_zero"], 1)
            up_body(0, True)
            with act.Fori(1, NUP) as i:
                up_body(i, False)
            silu_of(NUP - 1)
            act_hi_of(NUP - 1)

            def ssq_e(g):
                for t in range(2):
                    act.wait_ge(S["dn_sum"], 2 * g + t + 1)
                    if g + t:
                        act.wait_ge(S["ssf"], 2 * g + t)
                    act.activation(mraw2[:, 0, 0:512], xm[:, t, 512 * g:512 * g + 512], ACT.Square,
                                   accum_out=ss3[:, 4 * t + g:4 * t + g + 1]).then_inc(S["ssf"], 1)

            for l in range(88):
                round_sub(act, QE, l)
                if l in (24, 46):
                    g = l // 22 - 1
                    act.wait_ge(S["pe_done"], 4 * QE + 22 * (g + 1))
                    if g == 0:
                        act.wait_ge(S["act_ready"], NUP)
                    for t in range(2):
                        f(dr[:, g, t, :], ps[:, 2 * g + t, :], ACT.Copy, "dn_evac")
                if l in (48, 54, 72):
                    ssq_e({48: 0, 54: 1, 72: 2}[l])
            ssq_e(3)
            act.wait_ge(S["rsum"], 2)
            f(rs[:, 2:4], rs[:, 2:4], ACT.Sqrt, "rstd3", scale=1.0 / D, bias=eps[:, 0:1])
            act.wait_ge(S["rinv"], 1)
            f(xm[:, 0, :], xm[:, 0, :], ACT.Copy, "fin0", scale=rs[:, 2:3])

        @block.vector
        def _(dve):
            own = Own(dve, S["dve_own"])

            def sg_(ins, sem):
                ins.then_inc(S[sem], 1)

            def mod_unit(m):
                c, k = divmod(m, 16)
                src = (mraw if m < 96 else mraw2)[:, m % 2, :]
                dst = (acc if m < 96 else acc2)[:, c % 2, :]
                dve.wait_ge(MOD[m % 2], 16 * (m // 2 + 1))
                if k == 0:
                    if 2 <= c < 6:
                        dve.wait_ge(S["red_ps"], c - 1)
                    sg_(dve.tensor_scalar(dst, src, sc[:, 0, k:k + 1], None, ALU.mult), "mod_used")
                else:
                    dve.wait_ge(S["mod_used"], m)
                    sg_(dve.scalar_tensor_tensor(dst, src, sc[:, 0, k:k + 1], dst, ALU.mult, ALU.add), "mod_used")

            sg_(dve.memset(eps[:, :], EPS), "epsok")
            dve.wait_ge(S["vt_ps"], 7)
            sg_(dve.tensor_copy(vec[:, 0:252], ps[:, 3, 0:252]), "vt_sb")
            sg_(dve.tensor_copy(vec[:, 252:NV], ps[:, 4, 0:NV - 252]), "vt_sb")
            dve.wait_ge(S["vt_sb"], 2)
            dve.wait_ge(S["cv_hi"], 2)
            for j in range(2):
                sg_(dve.tensor_tensor(cvec[:, :, 2 * j + 1], sc[:, j, :], cvec[:, :, 2 * j].bitcast(F32), ALU.subtract),
                    "cv_ready")

            def sine_arg(src, b, sem):
                own(dve.tensor_scalar(sa[:, :], src, vec[0:HID, b:b + 1], vec[0:HID, V_FR:V_FR + 1], ALU.add, ALU.mult))
                own.wait()
                own(dve.tensor_scalar(sk[:, :], sa[:, :], 1.0 / (2 * np.pi), 12582912.0, ALU.mult, ALU.add))
                own.wait()
                own(dve.tensor_scalar(sk[:, :], sk[:, :], 12582912.0, None, ALU.subtract))
                own.wait()
                own(dve.scalar_tensor_tensor(sr[:, :], sk[:, :], -6.28125, sa[:, :], ALU.mult, ALU.add))
                own.wait()
                own(dve.scalar_tensor_tensor(sr[:, :], sk[:, :], 6.28125 - 2 * np.pi, sr[:, :], ALU.mult, ALU.add))
                own.wait()
                sg_(dve.tensor_scalar(sr[:, :], sr[:, :], 3.1415925, -3.1415925, ALU.min, ALU.max), sem)

            def turn_evac(t):
                dve.wait_ge(S["xn_ps"], t + 1)
                sg_(dve.tensor_copy(xn[:, t, :], ps[:, 4 + t % 4, 0:T]), "xn_dve")
                sg_(dve.tensor_copy(cn[:, t, :], ps[:, 4 + t % 4, T:2 * T]), "xn_dve")

            def rows_out(g):
                dve.wait_ge(S["pe_done"], 8 * (g + 1))
                if g >= 2:
                    dve.wait_ge(S["col_ps"], g - 1)
                sg_(dve.tensor_copy(rows4[:, g % 2, :], ps[0:4, g % 2, :]), "rows_sb")

            for g in range(8):
                for s in range(8):
                    l = 8 * g + s
                    if l % 4 != 3:
                        rest_sub(dve, QA, l)
                    if (g, s) == (0, 4):
                        dve.wait_ge(S["f1_ps"], 1)
                        sine_arg(ps[0:HID, 5, 0:T], V_B1, "f1_arg")
                    if (g, s) == (1, 0):
                        dve.wait_ge(S["f2_ps"], 1)
                        dve.wait_ge(S["f1_sb"], 1)
                        sine_arg(ps[0:HID, 6, 0:T], V_B2, "f2_arg")
                    if g >= 1 and s == 2:
                        rows_out(g - 1)
                    for j0, at_ in ((0, (1, 5)), (4, (2, 1))):
                        if (g, s) == at_:
                            for j in range(j0, j0 + 4):
                                t, c = divmod(j, 4)
                                dve.wait_ge(S["h3_ps"], j + 1)
                                sg_(dve.tensor_tensor(taps[:, t, 512 * c:512 * c + 512], ps[:, 4 + j % 4, :],
                                                      decay[:, t, 512 * (c % 2):512 * (c % 2) + 512], ALU.mult), "h3_sb")
                    if (g, s) == (2, 6):
                        dve.wait_ge(S["rstd_done"], 1)
                        own(dve.reciprocal(rs[:, 0:4], rs[:, 0:4]))
                        own.wait()
                        for j in range(4):
                            sg_(dve.tensor_scalar(diag[:, j, :], ident(), rs[:, j:j + 1], None, ALU.mult), "diag_ready")
                    if (g, s) in [(4, 3), (4, 5), (4, 7), (5, 1), (5, 3), (5, 5), (5, 7), (6, 0)]:
                        turn_evac(2 * [(4, 3), (4, 5), (4, 7), (5, 1), (5, 3), (5, 5), (5, 7), (6, 0)].index((g, s)) + 1)
            rows_out(7)
            dve.wait_ge(S["col_ps"], 8)
            for j in range(2):
                sg_(dve.tensor_tensor(mcol[:, j, :], ps[:, 2, j:64:2], vec[:, V_BM:V_BM + 32], ALU.add), "gx_ready")
            dve.wait_ge(S["gx_ready"], 2)
            for j in range(2):
                sg_(dve.scalar_tensor_tensor(gx[:, j, :], mcol[:, j, 16:32], 1.0, vec[:, V_GA:V_GA + 16], ALU.add, ALU.mult),
                    "gx_ready")
            dve.wait_ge(S["gx_ready"], 4)
            dve.wait_ge(S["xn_act"], KT)

            def operand_lo(t, src, dst, dst_hi, j, hi_sem, sem):
                b = 2 * j + t % 2
                if t >= 2:
                    dve.wait_ge(S[sem], t - 1)
                own(dve.tensor_scalar(hf[:, b, :], src[:, t, :], gx[:, j, t:t + 1], mcol[:, j, t:t + 1], ALU.mult, ALU.add))
                own.wait()
                dve.wait_ge(S[hi_sem], t + 1)
                sg_(dve.tensor_tensor(dst[:, t, :], hf[:, b, :], dst_hi[:, t, :].bitcast(F32), ALU.subtract), sem)

            def hy_sides(G):
                half, col, jg = HY[G]
                dst = {C_V: bv, C_X1: bx1, C_X0: bx0}[col]
                dve.wait_ge(S["mid_tap"], 2 * G + 2)
                if G == 9:
                    dve.wait_ge(S["red_ps"], 1)
                    sg_(dve.tensor_tensor(m2[:, 0:8], ps[:, 2, 256:264], vec[:, V_BM + 48:V_BM + 56], ALU.add), "red_sb")
                for jj in range(2):
                    o, src = dst[:, 2 * jg + jj, :], ps[:, 2 * (G % 2) + jj, :]
                    w = V_HC + col // P + 4 * half + 2 * jg + jj
                    own(dve.scalar_tensor_tensor(o[:, 1:T], src[:, 0:T - 1], vec[:, w:w + 1], o[:, 1:T], ALU.mult, ALU.add))
                for jj in range(2):
                    o, src = dst[:, 2 * jg + jj, :], ps[:, 2 * (G % 2) + jj, :]
                    w = V_HC + 48 + col // P + 4 * half + 2 * jg + jj
                    own.wait(1 - jj if jj == 0 else 0)
                    sg_(dve.scalar_tensor_tensor(o[:, 0:T - 1], src[:, 1:T], vec[:, w:w + 1], o[:, 0:T - 1], ALU.mult, ALU.add),
                        "hy_evac")

            def spectra_product(h):
                cs = slice(512 * h, 512 * h + 512)
                dve.wait_ge(S["dft_ps"], h + 1)
                t0, t1 = tt[:, 0, :], tt[:, 1, :]
                for f in range(2):
                    re, im = ps[:, 4 + f, :], ps[:, 6 + f, :]
                    own(dve.tensor_tensor(t0, re, kre[:, f, cs], ALU.mult))
                    own(dve.tensor_tensor(t1, im, kim[:, f, cs], ALU.mult))
                    own(dve.tensor_tensor(yf[:, 2 + f, :], re, kim[:, f, cs], ALU.mult))
                    own.wait(1)
                    own(dve.tensor_tensor(yf[:, f, :], t0, t1, ALU.subtract))
                    own.wait()
                    if f == 0:
                        own(dve.tensor_copy(yf[0:1, 0, :], t0[0:1, :]))
                        own.wait()
                    own(dve.tensor_tensor(t0, im, kre[:, f, cs], ALU.mult))
                    own.wait()
                    if f == 0:
                        own(dve.tensor_tensor(yf[:, 2, :], yf[:, 2, :], t0, ALU.add))
                        own.wait()
                        own(dve.tensor_copy(yf[0:1, 2, :], t1[0:1, :]))
                        own.wait()
                    else:
                        sg_(dve.tensor_tensor(yf[:, 3, :], yf[:, 3, :], t0, ALU.add), "cplx")

            def hyena(h, step):
                if step == 0:
                    spectra_product(h)
                if step == 1:
                    dve.wait_ge(S["y_ps"], h + 1)
                    for j in range(4):
                        sg_(dve.scalar_tensor_tensor(bv[:, j, :], bv[:, j, :], vec[:, V_HB + 4 * h + j:V_HB + 4 * h + j + 1],
                                                     ps[:, 4 + j // 2, T * (j % 2):T * (j % 2) + T], ALU.mult, ALU.add), "y2_done")
                if step == 2:
                    dve.wait_ge(S["hrt_done"], h + 1)
                    own(dve.reciprocal(rt[:, :, :], rt[:, :, :]))
                    own.wait()
                    for j in range(4):
                        sg_(dve.scalar_tensor_tensor(bv[:, j, :], bv[:, j, :], vec[:, V_HG + 4 * h + j:V_HG + 4 * h + j + 1],
                                                     rt[:, j, :], ALU.mult, ALU.mult), "hy_f32")

            def kv_evac(G):
                dve.wait_ge(S["pe_done"], 4 * quad_of(G) + 8)
                if G > G_KV:
                    dve.wait_ge(S["hy_mix"], 2)
                for b in (2, 3):
                    dst = ktok[:, b, :] if G == G_KV else vtok[:, b, 512 * (G - G_KV - 1):512 * (G - G_KV)]
                    ins = dve.tensor_copy(dst, ps[:, b, :])
                sg_(ins, "kv_dve")

            def red_out(c):
                dve.wait_ge(S["red_ps"], c + 1)
                sg_(dve.tensor_tensor(m2[:, 8 * c:8 * c + 8], ps[:, 7, 0:8], vec[:, V_BM + 48 + 8 * c:V_BM + 56 + 8 * c], ALU.add),
                    "red_sb")

            def log_gate(j):
                d, t = divmod(j, 4)
                dve.wait_ge(S["la_exp"], j + 1)
                sg_(dve.scalar_tensor_tensor(la[:, d, t, :], ps[:, 4 + j % 3, :], 0.0, ea[:, :], ALU.min, ALU.subtract), "la_done")

            def pair_in(p):
                dve.wait_ge(S["exps"], 4 * p + 4)
                for d in range(2):
                    sg_(dve.tensor_tensor(qe[:, d, :], qt[:, p, :], ep[:, d, :], ALU.mult), "pairs_in")
                for d in range(2):
                    sg_(dve.tensor_tensor(ke[:, d, :], ke[:, d, :], ps[:, 7, 0:T], ALU.mult), "pairs_in")

            def pair_mid(p):
                dve.wait_ge(S["u_ps"], 3 * p + 1)
                sg_(dve.tensor_copy(st[:, 0, 0, :], ps[:, 5, 3 * P:4 * P]), "states")
                sg_(dve.tensor_copy(st[:, 1, 3, :], ps[:, 6, 3 * P:4 * P]), "states")
                for k in range(3):
                    for d, c, nxt, e in ((0, k, k + 1, CH * k + CH - 1), (1, 3 - k, 2 - k, CH * (3 - k))):
                        b, slot = u_slot(d, c)
                        dve.wait_ge(S["states"], 8 * p + 2 * k + d + 1)
                        sg_(dve.scalar_tensor_tensor(st[:, d, nxt, :], st[:, d, c, :], ep[:, d, e:e + 1],
                                                     ps[:, b, P * slot:P * slot + P], ALU.mult, ALU.add), "states")
                n = 8 * p
                for hh in range(2):
                    dve.wait_ge(S["u_ps"], 3 * p + 2 + hh)
                    b = 7 if hh == 0 else 4
                    v = ps[:, b, :].rearrange("p (t d i) -> p t d i", t=2, d=2)
                    for k in (0, 1):
                        r = slice(CH * k, CH * k + CH)
                        sg_(dve.tensor_copy(scm[r, hh, :, r], v[r, :, 1, r]), "sc_set")
                    for k in (0, 1):
                        r = slice(CH * k, CH * k + CH)
                        n += 1
                        dve.wait_ge(S["sc_set"], n + k * 1)
                        sg_(dve.copy_predicated(scm[r, hh, :, r], mask[r, :, :], v[r, :, 0, r]), "sc_set")
                    n += 2

            def pair_norm(p):
                dve.wait_ge(S["grt_done"], p + 1)
                own(dve.reciprocal(grt[:, :, :], grt[:, :, :]))
                own.wait()
                sg_(dve.scalar_tensor_tensor(sg[:, 2 * p:2 * p + 2, :], ps[:, 5:7, 0:T], vec[:, V_GG:V_GG + 1], grt[:, :, :],
                                             ALU.mult, ALU.mult), "g_f32")

            def gla(slot):
                p, k = divmod(slot, 5)
                if p < 4:
                    if k == 0:
                        pair_in(p)
                    if k == 2:
                        pair_mid(p)
                    if k == 4:
                        pair_norm(p)
                if slot in PROD:
                    p = PROD[slot]
                    z = (2 * p + 2) % 8
                    dve.wait_ge(S["g_evac"], p + 1)
                    dve.wait_ge(S["g_f32"], p + 1)
                    sg_(dve.tensor_tensor(sg[:, 2 * p:2 * p + 2, :], sg[:, 2 * p:2 * p + 2, :], sg[:, z:z + 2, :], ALU.mult),
                        "g_prod")

            HYS = {(6, 1): (0, 0), (7, 1): (0, 1), (8, 2): (0, 2), (G_R, 1): (1, 0), (G_Q, 1): (1, 1), (G_Q + 1, 2): (1, 2)}
            for G in range(NGRP):
                for s in range(subs_of(G)):
                    if G == 0:
                        for t in range(4 * s, 4 * s + 4):
                            operand_lo(t, xn, hx_lo, hx_hi, 0, "hx_hi_ready", "hx_ready")
                    if s % 4 != 3:
                        rest_sub(dve, quad_of(G), s, 128 if G == G_R else 1024)
                    if G < 4:
                        operand_lo(4 * G + s, cn, hc_lo, hc_hi, 1, "hc_hi_ready", "hc_ready")
                    if 1 <= G <= G_R and s == 2:
                        hy_sides(G - 1)
                    if (G, s) in HYS:
                        hyena(*HYS[G, s])
                    if (G, s) == (G_Q, 2):
                        dve.wait_ge(S["pe_done"], 4 * (quad_of(G_R) + 1))
                        for b in range(2):
                            sg_(dve.tensor_copy(rT[0:32, T * b:T * b + T], ps[0:32, b, 0:T]), "rT_ready")
                    if (G, s) in ((G_Q + 1, 2), (G_Q + 2, 0)):
                        j = G - G_Q - 1
                        dve.wait_ge(S["pe_done"], 4 * (quad_of(G_Q + j) + 1))
                        b = 2 * ((G_Q + j) % 2)
                        sg_(dve.tensor_scalar(qt[:, 2 * j:2 * j + 2, :], ps[:, b:b + 2, 0:T], DK ** -0.5, None, ALU.mult), "q_evac")
                    if G_KV < G <= G_G and s == 0:
                        kv_evac(G - 1)
                    if (G, s) == (G_G, 0):
                        sg_(dve.memset(scm[:, :, :, :], 0.0), "scm_zero")
                        dve.wait_ge(S["scm_zero"], 1)
                    for m in MODS[G, s]:
                        mod_unit(m)
                    if G_KV <= G < G_G and s == 3:
                        red_out(1 + G - G_KV)
                    if (G, s) == (G_KV + 2, 3):
                        dve.wait_ge(S["red_sb"], 4)
                        own(dve.scalar_tensor_tensor(g2[:, :], m2[:, 16:32], 1.0, vec[:, V_GF:V_GF + 16], ALU.add, ALU.mult))
                    if G == G_KV + 1 and s >= 1:
                        log_gate(s - 1)
                    if (G, s) == (G_KV + 2, 0):
                        log_gate(7)
                    if G >= G_G:
                        gla(4 * (G - G_G) + s)

            def residual(g, gate, src, tmp, evac, done, get):
                cs = slice(512 * g, 512 * g + 512)
                for t in range(2):
                    sg_(dve.tensor_tensor(tmp[:, t, :], src(t), gate[:, cs], ALU.mult), evac)
                for t in range(2):
                    dve.wait_ge(S[evac], get + 1 + t)
                    sg_(dve.tensor_tensor(xm[:, t, cs], xm[:, t, cs], tmp[:, t, :], ALU.add), done)

            def wo_out(g):
                dve.wait_ge(S["pe_done"], 4 * QC + 8 * (g + 1))
                dve.wait_ge(S["x_again"], 16)
                dve.wait_ge(S["ga_ready"], 1)
                residual(g, gab, lambda t: ps[:, 2 * (g % 2) + t, :], wt, "wo_evac", "xm_done", 2 * g)

            for g in range(4):
                for s in range(8):
                    if s % 4 != 3:
                        rest_sub(dve, QC + 2 * g, s)
                    if g == 0:
                        gla(16 + s)
                    if (g, s) == (0, 7):
                        dve.wait_ge(S["ga_ps"], 1)
                        dve.wait_ge(S["ga_bias"], 16)
                        sg_(dve.tensor_tensor(gab[:, :], ps[:, 4:8, :].rearrange("p a b -> p (a b)"), gab[:, :], ALU.add), "ga_ready")
                    if g >= 1 and s == 2:
                        wo_out(g - 1)
            wo_out(3)
            dve.wait_ge(S["ssm"], 8)
            sg_(dve.tensor_reduce(rs[:, 0:2], ss[:, :].rearrange("p (t g) -> p t g", t=2), AXX, ALU.add), "rsum")
            dve.wait_ge(S["rstd2"], 1)
            own(dve.reciprocal(rs[:, 0:2], rs[:, 0:2]))
            own.wait()
            for t in range(2):
                sg_(dve.tensor_scalar(dg[:, t, :], ident(), rs[:, t:t + 1], None, ALU.mult), "dg2")

            def h2_lo(j):
                dve.wait_ge(S["h2_hi"], j + 1)
                sg_(dve.tensor_tensor(hx_lo[:, 2 * j:2 * j + 2, :], h2f[:, j % 2, :, :],
                                      hx_hi[:, 2 * j:2 * j + 2, :].bitcast(F32), ALU.subtract), "h2_ready")

            for j in range(8):
                dve.wait_ge(S["xt_ps"], j + 1)
                if j >= 2:
                    dve.wait_ge(S["h2_ready"], j - 1)
                for i in range(2):
                    k = 2 * j + i
                    sg_(dve.tensor_scalar(h2f[:, j % 2, i, :], ps[:, 4 + j % 4, T * i:T * i + T], g2[:, k:k + 1],
                                          m2[:, k:k + 1], ALU.mult, ALU.add), "h2_f32")
                if j:
                    h2_lo(j - 1)
            h2_lo(7)

            taps_ff = vec[:, V_FC:NV].rearrange("p (k f) -> p k f", k=9)

            def gate_of(i):
                dve.wait_ge(S["pe_done"], (QD + i * 2) * 4 + 8)
                dve.wait_ge(S["silu_done"], i + 1)
                dve.wait_ge(S["act_ready"], i)
                sg_(dve.tensor_tensor(a32[:, :, :], ps[:, 2:4, 0:T], cv[:, :, :], ALU.mult), "act_f32")

            def act_lo_of(i):
                dve.wait_ge(S["act_h"], i + 1)
                sg_(dve.tensor_tensor(act_lo[:, bass.ds(i * 2, 2), :], a32[:, :, :],
                                      act_hi[:, bass.ds(i * 2, 2), :].bitcast(F32), ALU.subtract), "act_ready")

            K_OWN = 18
            before = own.n

            def conv(i, base):
                c = Own(dve, S["dve_own"], base)
                c(dve.tensor_copy(cwi[:, :, :], taps_ff[:, :, bass.ds(i * 2, 2)]))
                c.wait()
                dve.wait_ge(S["a_evac"], i * 2 + 2)
                img = [cv[:, j, :].rearrange("p (y x) -> p y x", y=4) for j in range(2)]
                for j in range(2):
                    c(dve.tensor_scalar(img[j], ap[:, j, :, 1:65], cwi[:, 4, j:j + 1], None, ALU.mult))
                order = [k for k in range(9) if k != 4]
                for k in order:
                    dy, dx = k // 3 - 1, k % 3 - 1
                    y0, y1 = max(0, -dy), 4 - max(0, dy)
                    for j in range(2):
                        c.wait(1)
                        ins = dve.scalar_tensor_tensor(img[j][:, y0:y1, :], ap[:, j, y0 + dy:y1 + dy, 1 + dx:65 + dx],
                                                       cwi[:, k, j:j + 1], img[j][:, y0:y1, :], ALU.mult, ALU.add)
                        if (k, j) == (8, 1):
                            sg_(ins, "conv_done")
                        else:
                            c(ins)
                assert c.n == K_OWN, c.n

            def up_body(i, first):
                q = QD + i * 2
                for s in range(8):
                    if s % 4 != 3:
                        rest_sub(dve, q, s)
                    if s == 2 and not first:
                        gate_of(i - 1)
                    if s == 4 and not first:
                        act_lo_of(i - 1)
                    if s == 6:
                        conv(i, i * K_OWN + before)

            up_body(0, True)
            with dve.Fori(1, NUP) as i:
                up_body(i, False)
            gate_of(NUP - 1)
            act_lo_of(NUP - 1)

            def fin_mul(g, eng):
                cs = slice(512 * g, 512 * g + 512)
                eng.wait_ge(S["ssf"], 2 * g + 2)
                for t in range(2):
                    eng.tensor_tensor(xm[:, t, cs], xm[:, t, cs], gfin[:, cs], ALU.mult).then_inc(S["xg"], 1)

            def dn_out(g):
                if g < 2:
                    dve.wait_ge(S["dn_evac"], 2 * g + 2)
                    src = lambda t: dr[:, g, t, :]
                else:
                    dve.wait_ge(S["pe_done"], 4 * QE + 22 * (g + 1))
                    src = lambda t: ps[:, 2 * (g % 2) + t, :]
                residual(g, gfb, src, ft_, "dn_mul", "dn_sum", 2 * g)

            for l in range(88):
                if l % 4 != 3:
                    rest_sub(dve, QE, l)
                for m in DMODS.get(l, []):
                    mod_unit(m)
                if l == 42:
                    dve.wait_ge(S["gf_ps"], 1)
                    dve.wait_ge(S["gf_bias"], 16)
                    sg_(dve.tensor_tensor(gfb[:, :], ps[:, 4:8, :].rearrange("p a b -> p (a b)"), gfb[:, :], ALU.add), "gf_ready")
                    dve.wait_ge(S["gf_ready"], 1)
                if l in (46, 52, 70):
                    dn_out({46: 0, 52: 1, 70: 2}[l])
            dn_out(3)
            fin_mul(3, dve)
            sg_(dve.tensor_reduce(rs[:, 2:4], ss3[:, :].rearrange("p (t g) -> p t g", t=2), AXX, ALU.add), "rsum")
            dve.wait_ge(S["rstd3"], 1)
            sg_(dve.reciprocal(rs[:, 2:4], rs[:, 2:4]), "rinv")
            dve.wait_ge(S["rinv"], 1)
            dve.wait_ge(S["xg"], 8)
            sg_(dve.tensor_scalar(xm[:, 1, :], xm[:, 1, :], rs[:, 3:4], None, ALU.mult), "fin1")

        @block.gpsimd
        def _(pool):
            def sg_(ins, sem):
                ins.then_inc(S[sem], 1)

            sg_(pool.memset(pack[:, 0, :], 0.0), "row0")
            sg_(pool.memset(cvec[:, :, :].bitcast(F32), 0.0), "cv_zero")
            for g in range(8):
                for s in (3, 7):
                    rest_sub(pool, QA, 8 * g + s)
                    if (g, s) == (2, 3):
                        pool.wait_ge(S["h3_sb"], 8)
                        sg_(pool.memset(taps[0:1, 0, HYW:2 * HYW], 0.0), "row0")
                        pool.wait_ge(S["row0"], 2)
                        sg_(pool.tensor_tensor(hsum[:, :, :], taps[:, :, 0:HYW], taps[:, :, HYW:2 * HYW], ALU.add), "sd_done")
                    if (g, s) == (2, 7):
                        sg_(pool.tensor_tensor(hdif[:, :, :], taps[:, :, 0:HYW], taps[:, :, HYW:2 * HYW], ALU.subtract), "sd_done")

            PSTEP = {(4, 3): (0, 0), (7, 3): (0, 1), (8, 3): (0, 2), (10, 3): (1, 0), (G_Q, 3): (1, 1), (G_Q + 1, 3): (1, 2)}

            def hyena(h, step):
                if step == 0:
                    pool.wait_ge(S["hy_evac"], 20 if h else 8)
                    sg_(pool.tensor_tensor(bv[:, :, :], bv[:, :, :], bx1[:, :, :], ALU.mult), "z_done")
                if step == 1:
                    pool.wait_ge(S["y2_done"], 4 * (h + 1))
                    pool.wait_ge(S["hy_evac"], 24 if h else 12)
                    sg_(pool.tensor_tensor(bv[:, :, :], bv[:, :, :], bx0[:, :, :], ALU.mult), "y3_done")
                if step == 2:
                    pool.wait_ge(S["hy_hi"], h + 1)
                    sg_(pool.tensor_tensor(hm_lo[:, 4 * h:4 * h + 4, :], bv[:, :, :],
                                           hm_hi[:, 4 * h:4 * h + 4, :].bitcast(F32), ALU.subtract), "hy_mix")

            def gla(slot):
                p, k = divmod(slot, 5)
                if k == 0 and p < 4:
                    pool.wait_ge(S["exps"], 4 * p + 4)
                    cs = slice(P * p, P * p + P)
                    for d in range(2):
                        sg_(pool.tensor_tensor(kd[:, d, :, :], kd[:, d, :, :], ktok[:, 0:2, cs], ALU.mult), "kdc")
                        sg_(pool.tensor_tensor(kc[:, d, :, :], kc[:, d, :, :], ktok[:, 2:4, cs], ALU.mult), "kdc")
                if slot - 1 in PROD:
                    p = PROD[slot - 1]
                    pool.wait_ge(S["g_hi"], p + 1)
                    sg_(pool.tensor_tensor(gm_lo[:, 2 * p:2 * p + 2, :], sg[:, 2 * p:2 * p + 2, :],
                                           gm_hi[:, 2 * p:2 * p + 2, :].bitcast(F32), ALU.subtract), "g_mix")

            for G in range(NGRP):
                for s in range(subs_of(G)):
                    if s % 4 == 3:
                        rest_sub(pool, quad_of(G), s, 128 if G == G_R else 1024)
                    if (G, s) in PSTEP:
                        hyena(*PSTEP[G, s])
                    if (G, s) == (G_R, 3):
                        pool.wait_ge(S["cplx"], 2)
                        sg_(pool.memset(wg[:, :, :], 0.0), "wg_zero")
                        pool.wait_ge(S["wg_zero"], 1)
                        sg_(pool.memset(rT[32:33, :], 1.0), "rT_one")
                        pool.wait_ge(S["rT_one"], 1)
                    if G >= G_G:
                        gla(4 * (G - G_G) + s)
            for g in range(4):
                for s in range(8):
                    if s % 4 == 3:
                        rest_sub(pool, QC + 2 * g, s)
                    if g == 0:
                        gla(16 + s)
            pool.wait_ge(S["ssm"], 8)
            sg_(pool.memset(ap[:, :, :, :], 0.0), "ap_zero")
            with pool.Fori(0, NUP) as i:
                rest_sub(pool, QD + i * 2, 3)
                rest_sub(pool, QD + i * 2, 7)
            for l in range(3, 88, 4):
                rest_sub(pool, QE, l)
                if l in (51, 59, 79):
                    g = {51: 0, 59: 1, 79: 2}[l]
                    cs = slice(512 * g, 512 * g + 512)
                    pool.wait_ge(S["gfin_in"], 16)
                    pool.wait_ge(S["ssf"], 2 * g + 2)
                    for t in range(2):
                        sg_(pool.tensor_tensor(xm[:, t, cs], xm[:, t, cs], gfin[:, cs], ALU.mult), "xg")


def constants():
    n = np.arange(P)
    same = (n[:, None] // CH) == (n[None, :] // CH)
    r, c = n[:, None], n[None, :]
    g = 1.0 / 16.0
    con = np.zeros((P, 10, P), np.float32)
    con[:, K_ID] = np.eye(P)
    con[:, K_MEAN] = 1.0 / P
    con[:, K_ONE] = 1.0
    con[:, K_TF] = g * (same & (r <= c))
    con[:, K_TB] = g * (same & (r >= c))
    con[:, K_SF] = g * (same & (r > c))
    con[:, K_SB] = g * (same & (r < c))
    con[:, K_SC] = g * (r > c)
    con[:, K_PC] = g * (r < c)
    con[:, K_AL] = g
    m = (np.arange(CH)[None, :] >= (n[:, None] % CH)).astype(np.int32)
    L = 2 * T
    t, f = np.arange(T)[:, None], np.arange(T)[None, :]
    ang = 2 * np.pi * ((t * f) % L) / L
    fw = np.concatenate([np.cos(ang), -np.sin(ang)], axis=1)
    fw[:, T] = (-1.0) ** np.arange(T)
    iv = np.concatenate([2 * np.cos(ang.T), -2 * np.sin(ang.T)], axis=0) / L
    iv[0] = 1.0 / L
    iv[T] = ((-1.0) ** np.arange(T)) / L
    pos = np.arange(T)
    tn = pos / (T - 1)
    a2 = (2 * np.pi / T) * ((pos[:, None] * np.arange(1, BANDS + 1)[None, :]) % T)
    z = np.concatenate([tn[:, None], np.cos(a2), np.sin(a2)], axis=1)
    deltas = np.abs(np.linspace(np.log(1e-2) / 1.5, np.log(1e-2) / 0.3, HYW))
    dec = np.exp(-tn[:, None] * deltas[None, :])

    def tiles(x):
        return np.ascontiguousarray(x.reshape(-1, P, x.shape[1]).transpose(1, 0, 2).reshape(P, -1), np.float32)

    return {
        "con": con.reshape(P, -1), "mask": np.tile(m, (1, 2)), "sel": np.array([[1, 0], [1, 0], [0, 1], [0, 1]], np.float32),
        "fwd": tiles(fw), "inv": tiles(iv), "decay": tiles(dec), "zfeat": np.ascontiguousarray(z.T, np.float32),
    }


NAMES = ["x", "c", "ctx", "c_ctx", "w_mod", "b_mod", "g_attn", "w_in", "hy_conv", "hy_w1", "hy_b1", "hy_freq", "hy_w2", "hy_b2",
         "hy_w3", "hy_bias", "hy_out_g", "gla_wg_f", "gla_bg_f", "gla_wg_b", "gla_bg_b", "gla_out_g", "w_out", "g_ffn",
         "ffn_w_up", "ffn_conv", "ffn_w_down", "g_final"]


def kernel(**inputs):
    import concourse.bacc as bacc
    from concourse.bass_utils import run_bass_kernel_spmd

    nc = bacc.Bacc("TRN2", target_bir_lowering=False, num_devices=1)
    data = {k: np.ascontiguousarray(inputs[k]) for k in NAMES}
    data.update(constants())
    arrays, aps = {}, {}
    for k, v in data.items():
        arrays[f"in_{k}"] = v
        aps[k] = nc.dram_tensor(f"in_{k}", v.shape, mybir.dt.from_np(v.dtype), kind="ExternalInput").ap()
    out = nc.dram_tensor("out_0", (1, T, D), F32, kind="ExternalOutput").ap()
    build(nc, aps, out)
    return run_bass_kernel_spmd(nc, [arrays], core_ids=[0]).results[0]["out_0"]
```

```python
from contextlib import ExitStack

import numpy as np

import concourse.bass as bass
from concourse import mybir

ALU = mybir.AluOpType
ACT = mybir.ActivationFunctionType
AXX = mybir.AxisListType.X
F32 = mybir.dt.float32
F32R = mybir.dt.float32r
I32 = mybir.dt.int32

P = 128
D = 2048
T = 256
KT = D // P
HYW = 1024
HEADS, DK, DV, CH = 8, 64, 128, 64
RANK = 16
FF = 5632
FT = FF // P
EPS = 1e-6
GRID_W = 64
NB, BANDS, HID = 33, 16, 64

C_X0, C_X1, C_V = 0, HYW, 2 * HYW
C_K = 3 * HYW
C_GV = C_K + HEADS * DK
C_R = C_GV + HEADS * DV
C_Q = C_R + 2 * RANK
C_G = C_Q + HEADS * DK

HY = []
for half in range(2):
    order = (C_V, C_X1, C_X0) if half == 0 else (C_X1, C_V, C_X0)
    for col in order:
        for j in range(2):
            HY.append((half, col, j))
G_R, G_Q, G_KV, G_G = 12, 13, 15, 18
NGRP = 22

RING = 6

QA, QB = 0, 16
def quad_of(G):
    if G < G_KV:
        return QB + G
    if G < G_G:
        return QB + G_KV + 2 * (G - G_KV)
    return QB + G_KV + 6 + (G - G_G)
QC = quad_of(NGRP - 1) + 1
QD = QC + 8
QE = QD + 2 * (FT // 2)
QEND = QE + 22
NUP = FT // 2
NGATE = KT

V_C, V_CC, V_GA, V_GF, V_HB, V_HG, V_GG, V_FR, V_B1, V_B2 = 0, 16, 32, 48, 64, 72, 80, 81, 82, 83
V_BM, V_HC, V_FC = 84, 180, 252
NV = V_FC + 9 * FT

(K_ID, K_MEAN, K_ONE, K_TF, K_TB, K_SF, K_SB, K_SC, K_PC, K_AL) = range(10)


def subs_of(G):
    return 8 if G_KV <= G < G_G else 4


def slot_of(n):
    if n < 4 * QD:
        return (n - 4 * QD) % RING
    if n < 4 * QE:
        return (n - 4 * QD) % 4
    return (n - 4 * QE + 4) % RING


def earlier(n):
    return [m for m in range(n) if slot_of(m) == slot_of(n)]


def mod_units(G, s):
    if G < G_R:
        return s % 2
    if G == G_R:
        return 0
    return 2 if G_KV <= G < G_G else 1


class Own:

    def __init__(self, eng, sem, base=0):
        self.eng, self.sem, self.n, self.base = eng, sem, 0, base

    def __call__(self, ins):
        ins.then_inc(self.sem, 1)
        self.n += 1
        return ins

    def wait(self, back=0):
        self.eng.wait_ge(self.sem, self.base + self.n - back)


def build(nc, a, out):
    with ExitStack() as ctx:
        BASE = 16512

        def at(name, kb, shape, dt=F32):
            return nc.alloc_sbuf_tensor_at(name, shape, dt, offset=BASE + int(kb * 1024))

        raw = at("raw", 0, [P, RING, 1024])
        lo = at("lo", 0, [P, RING, 1024], F32R)
        hi = at("hi", 24, [P, RING, 1024], F32R)
        hx_hi = at("hx_hi", 48, [P, KT, T], F32R)
        hx_lo = at("hx_lo", 64, [P, KT, T], F32R)
        hc_hi = at("hc_hi", 80, [P, KT, T], F32R)
        hc_lo = at("hc_lo", 96, [P, KT, T], F32R)
        mraw = at("mraw", 112, [P, 2, 1024])
        acc = at("acc", 120, [P, 2, 1024])
        vec = at("vec", 128, [P, NV])
        mcol = at("mcol", 130.75, [P, 2, 32])
        gx = at("gx", 131, [P, 2, 16])
        m2 = at("m2", 131.25, [P, 32])
        g2 = at("g2", 131.5, [P, 16])
        sc = at("sc", 131.625, [P, 2, 16])
        ss = at("ss", 131.75, [P, 8])
        rs = at("rs", 131.875, [P, 4])
        ss3 = at("ss3", 132, [P, 8])
        eps = at("eps", 132.125, [P, 1])
        con = at("con", 132.25, [P, 10, P])
        mask = at("mask", 137.25, [P, 2, CH], I32)
        sel = at("sel", 137.75, [4, 2])
        xtok = at("xtok", 48, [P, 2, D])
        ctok = at("ctok", 64, [P, 2, D])
        cvec = at("cvec", 80, [P, KT, P], F32R)
        w3 = at("w3", 88, [HID, 2 * HYW])
        diag = at("diag", 88, [P, 4, P])
        decay = at("decay", 96, [P, 2, HYW])
        pack = at("pack", 104, [P, 7, P])
        fwd_a = at("fwd_a", 108, [P, 2, 512])
        taps = at("taps", 112, [P, 2, 2 * HYW])
        xn = at("xn", 138, [P, KT, T])
        cn = at("cn", 154, [P, KT, T])
        junk = at("junk", 138, [P, D])
        hsum = at("hsum", 170, [P, 2, HYW])
        hdif = at("hdif", 178, [P, 2, HYW])
        rows4 = at("rows4", 186, [4, 2, 512])
        zf = at("zf", 190, [NB, T])
        w1 = at("w1", 191, [NB, HID])
        w2 = at("w2", 191.5, [HID, HID])
        sa = at("sa", 192, [HID, T])
        sk = at("sk", 193, [HID, T])
        sr = at("sr", 194, [HID, T])
        h1 = at("h1", 195, [HID, T])
        h2 = at("h2", 196, [HID, T])
        fwd = at("fwd", 138, [P, 2, 512])
        inv = at("inv", 142, [P, 4, T])
        bv = at("bv", 146, [P, 4, T])
        bx1 = at("bx1", 150, [P, 4, T])
        bx0 = at("bx0", 154, [P, 4, T])
        zt = at("zt", 158, [P, 2, 512])
        yf = at("yf", 162, [P, 4, 512])
        sq = at("sq", 162, [P, 4, T])
        rt = at("rt", 166, [P, 4, T])
        tt = at("tt", 170, [P, 2, 512])
        hf = at("hf", 170, [P, 4, T])
        hm_hi = at("hm_hi", 174, [P, 8, T], F32R)
        hm_lo = at("hm_lo", 182, [P, 8, T], F32R)
        kre = at("kre", 190, [P, 2, HYW])
        kim = at("kim", 198, [P, 2, HYW])
        ktok = at("ktok", 190, [P, 4, 512])
        vtok = at("vtok", 138, [P, 4, HEADS * DV])
        la = at("la", 154, [P, 2, 4, 512])
        qt = at("qt", 170, [P, 4, T])
        rT = at("rT", 198, [NB, 512])
        wg = at("wg", 200, [NB, 2, 512])
        ea = at("ea", 204, [P, 512])
        ep = at("ep", 198, [P, 2, T])
        ke = at("ke", 200, [P, 2, T])
        kd = at("kd", 202, [P, 2, 2, P])
        kc = at("kc", 204, [P, 2, 2, P])
        gm_hi = at("gm_hi", 80, [P, 8, T], F32R)
        gm_lo = at("gm_lo", 88, [P, 8, T], F32R)
        sg = at("sg", 96, [P, 8, T])
        st = at("st", 104, [P, 2, 4, P])
        qe = at("qe", 108, [P, 2, T])
        scm = at("scm", 110, [P, 2, 2, P])
        gsq = at("gsq", 204, [P, 2, T])
        grt = at("grt", 200, [P, 2, T])
        gt = at("gt", 202, [P, 2, T])
        xm = at("xm", 138, [P, 2, D])
        gab = at("gab", 154, [P, D])
        wt = at("wt", 162, [P, 2, 512])
        dg = at("dg", 166, [P, 2, P])
        h2f = at("h2f", 167, [P, 2, 2, T])
        sqj = at("sqj", 198, [P, 512])
        act_hi = at("act_hi", 154, [P, FT, T], F32R)
        act_lo = at("act_lo", 80, [P, FT, T], F32R)
        ap = at("ap", 198, [P, 2, 4, 66])
        cv = at("cv", 200.25, [P, 2, T])
        a32 = at("a32", 202.25, [P, 2, T])
        cwi = at("cwi", 204.25, [P, 9, 2])
        graw = at("graw", 16, [P, D])
        gacc = at("gacc", 40, [P, D])
        gsc = at("gsc", 132.1875, [P, 1])
        ssj = at("ssj", 48, [P, 512])
        gfb = at("gfb", 64, [P, D])
        gfin = at("gfin", 72, [P, D])
        dr = at("dr", 198, [P, 2, 2, 512])
        ft_ = at("ft_", 124, [P, 2, 512])

        ps = ctx.enter_context(nc.psum_tensor("ps", [P, 8, 512], F32))

        names = """conds ident_in packed packed1 packed2 consts_in sel_in mask_in x_in0 x_in1 ctx_in0 ctx_in1 fload w3_in decay_in fwd_in tables raw0 raw1 raw2 raw3 raw4 raw5 hi_ready lo_dve lo_pool pe_done
            mod_in0 mod_in1 mod_used gate_in gate_scale gate_used act_own dve_own 
            vt_ps cond_sb vt_sb sc_done cv_hi cv_zero cv_ready  rows_sb col_ps
            sq_done rstd_done diag_ready xn_ps xn_act xn_dve
            f1_ps f1_arg f1_sb f2_ps f2_arg f2_sb h3_ps h3_sb row0 sd_done kf_ps kf_sb
            gx_ready hx_f32 hx_pool hx_hi_ready hx_ready hc_hi_ready hc_ready  mid_tap hy_evac z_done zt_ps zt_sb dft_ps cplx y_ps y2_done
            y3_done hsq_done hms_ps hln gln hrt_done hy_f32 hy_hi hy_mix  q_evac kv_act kv_dve g_evac red_ps red_sb
            wg_zero wg_in rT_ready rT_one la_ps la_exp la_done cum_ps exps pairs_in kdc u_ps sc_set states o_ps gsq_done gms_ps grt_done g_f32 g_prod g_hi g_mix scm_zero
            x_again ga_bias ga_ps ga_ready  wo_evac xm_done ssm rstd2 dg2 xt_ps h2_f32 h2_hi h2_ready
            ap_zero  a_evac conv_done silu_done act_f32 act_h act_ready
            gfin_in gf_bias gf_ps gf_ready  dn_evac dn_sum ssf rstd3 rinv rsum dn_mul xg epsok fin0 fin1 out_done""".split()
        S = {n: ctx.enter_context(nc.semaphore(n)) for n in names}
        RAW = [S[f"raw{i}"] for i in range(RING)]
        MOD = [S["mod_in0"], S["mod_in1"]]

        w_mod, w_in, w_out = a["w_mod"][0], a["w_in"][0], a["w_out"][0]
        w_up, w_down, b_mod = a["ffn_w_up"][0], a["ffn_w_down"][0], a["b_mod"][0]

        def piece(w, k0, kn, c0, cn):
            cols = slice(c0, c0 + cn) if isinstance(c0, int) else bass.ds(c0, cn)
            return w[k0 * P:(k0 + kn) * P, cols].rearrange("(t p) c -> p t c", p=P)

        def ident(n=P):
            return con[0:n, K_ID, 0:n]

        def u_slot(d, c):
            return (5, {(0, 0): 0, (0, 2): 1, (1, 2): 2}[d, c]) if c % 2 == 0 else (6, {(0, 1): 0, (1, 1): 1, (1, 3): 2}[d, c])

        L_OUT, L_SPEC, L_NYQ, L_TURN, LAG = 10, 23, 39, 41, 3

        block = ctx.enter_context(nc.Block())

        def place(q, l):
            if isinstance(q, int):
                n = 4 * q + l
                return slot_of(n), len(earlier(n)) + 1
            r = l % 4
            return r, (q - QD) + l // 4 + len(earlier(4 * QD + r)) + 1

        def load_sub(sp, q, l, src, kn, cn):
            r, _ = place(q, l)
            if not isinstance(q, int):
                sp.wait_ge(S["pe_done"], q * 4 + l - 3)
            elif earlier(4 * q + l):
                sp.wait_ge(S["pe_done"], earlier(4 * q + l)[-1] + 1)
            sp.dma_start(raw[:, r, 0:kn * cn].rearrange("p (t c) -> p t c", t=kn), src).then_inc(RAW[r], 16)

        def round_sub(act, q, l, n=1024):
            r, count = place(q, l)
            act.wait_ge(RAW[r], count * 16)
            act.activation(hi[:, r, 0:n], raw[:, r, 0:n], ACT.Copy).then_inc(S["hi_ready"], 1)

        def rest_sub(eng, q, l, n=1024):
            r, _ = place(q, l)
            eng.wait_ge(S["hi_ready"], (q + l // 4) * 4 + l % 4 + 1)
            eng.tensor_tensor(lo[:, r, 0:n], raw[:, r, 0:n], hi[:, r, 0:n].bitcast(F32), ALU.subtract)\
                .then_inc(S["lo_dve" if l % 4 < 3 else "lo_pool"], 1)

        def hi_in(pe, q, l):
            pe.wait_ge(S["hi_ready"], (q + l // 4) * 4 + l % 4 + 1)

        def lo_in(pe, q, l):
            r, b = l % 4, q + l // 4
            if r < 3:
                pe.wait_ge(S["lo_dve"], b * 3 + r + 1)
            else:
                pe.wait_ge(S["lo_pool"], b + 1)

        def mod_chunk(m):
            return (3 * D, 3 * D + 1024, 4 * D, 4 * D + 1024, 2 * D, 2 * D + 1024, 5 * D, 5 * D + 1024)[m // 16]

        def mod_at():
            m, where = 0, {}
            for G in range(NGRP):
                for s in range(subs_of(G)):
                    where[G, s] = list(range(m, m + mod_units(G, s)))
                    m += mod_units(G, s)
            assert m == 96, m
            return where

        MODS = mod_at()

        def sub_src(G, s):
            if G < G_R:
                half, col, j = HY[G]
                return piece(w_in, 4 * s, 4, col + 512 * half + 256 * j, 256), 4, 256
            if G == G_R:
                return piece(w_in, 4 * s, 4, C_R, 2 * RANK), 4, 2 * RANK
            if G < G_KV:
                return piece(w_in, 4 * s, 4, C_Q + 256 * (G - G_Q), 256), 4, 256
            if G < G_G:
                return piece(w_in, 2 * s, 2, C_K + 512 * (G - G_KV), 512), 2, 512
            return piece(w_in, 4 * s, 4, C_G + 256 * (G - G_G), 256), 4, 256

        @block.sync
        def _(sp):
            def row(v, n):
                return v.rearrange("(a n) -> a n", n=n)

            def a_sub(l):
                load_sub(sp, QA, l, piece(w_mod, 2 * (l % 8), 2, 512 * (l // 8), 512), 2, 512)

            tables = a["con"].rearrange("p (k n) -> p k n", k=10)
            sp.dma_start(con[:, K_ID, :], tables[:, K_ID, :]).then_inc(S["ident_in"], 16)
            sp.wait_ge(S["row0"], 1)
            for r0, v in ((V_C, a["c"][0]), (V_CC, a["c_ctx"])):
                sp.dma_start(pack[r0:r0 + 16, 0, :], row(v, P)).then_inc(S["conds"], 16)
            a_sub(0)
            a_sub(1)
            for r0, v in ((V_GA, a["g_attn"][0]), (V_GF, a["g_ffn"][0]), (V_HB, a["hy_bias"][0]),
                          (V_HG, a["hy_out_g"][0]), (V_GG, a["gla_out_g"][0])):
                n = v.shape[0] // P
                sp.dma_start(pack[r0:r0 + n, 0, :], row(v, P)).then_inc(S["packed"], 16)
            a_sub(2)
            for r0, v in ((V_FR, a["hy_freq"]), (V_B1, a["hy_b1"]), (V_B2, a["hy_b2"])):
                sp.dma_start(pack[r0:r0 + 1, 0, 0:HID], v).then_inc(S["packed"], 16)
            a_sub(3)
            sp.dma_start(zf[:, :], a["zfeat"]).then_inc(S["fload"], 16)
            sp.dma_start(w1[:, :], a["hy_w1"][0]).then_inc(S["fload"], 16)
            sp.dma_start(w2[:, :], a["hy_w2"][0]).then_inc(S["fload"], 16)
            sp.dma_start(sel[:, :], a["sel"]).then_inc(S["sel_in"], 16)
            fc = a["ffn_conv"][0].rearrange("y x (a n) -> (y x a) n", n=P)
            for l in range(4, 64):
                a_sub(l)
                if l == 6:
                    sp.dma_start(w3[:, :], a["hy_w3"][0]).then_inc(S["w3_in"], 16)
                if l == 9:
                    sp.dma_start(decay[:, :, :], a["decay"].rearrange("p (t c) -> p t c", t=2)).then_inc(S["decay_in"], 16)
                if l == 13:
                    sp.dma_start(pack[0:96, 1, :], row(b_mod, P)).then_inc(S["packed1"], 16)
                    sp.dma_start(pack[0:72, 2, :], a["hy_conv"][0].rearrange("k (a n) -> (k a) n", n=P)).then_inc(S["packed1"], 16)
                if 14 <= l < 18:
                    i = l - 14
                    sp.dma_start(pack[0:99, 3 + i, :], fc[99 * i:99 * i + 99, :]).then_inc(S["packed1" if i < 2 else "packed2"], 16)
                if l == 19:
                    sp.dma_start(fwd_a[:, :, :], a["fwd"].rearrange("p (t c) -> p t c", t=2)).then_inc(S["fwd_in"], 16)
                if l in (23, 26):
                    t = (l - 23) // 3
                    sp.dma_start(xtok[:, t, :], a["x"][0][P * t:P * t + P]).then_inc(S[f"x_in{t}"], 16)
                if l in (29, 32):
                    t = (l - 29) // 3
                    sp.dma_start(ctok[:, t, :], a["ctx"][0][P * t:P * t + P]).then_inc(S[f"ctx_in{t}"], 16)
                if l == 36:
                    sp.dma_start(con[:, 1:10, :], tables[:, 1:10, :]).then_inc(S["consts_in"], 16)
                    sp.dma_start(mask[:, :, :], a["mask"].rearrange("p (t c) -> p t c", t=2)).then_inc(S["mask_in"], 16)

            for G in range(NGRP):
                for s in range(subs_of(G)):
                    src, kn, cn = sub_src(G, s)
                    load_sub(sp, quad_of(G), s, src, kn, cn)
                    for m in MODS[G, s]:
                        if m >= 2:
                            sp.wait_ge(S["mod_used"], m - 1)
                        sp.dma_start(mraw[:, m % 2, :], w_mod[(m % 16) * P:(m % 16 + 1) * P,
                                                              mod_chunk(m):mod_chunk(m) + 1024]).then_inc(MOD[m % 2], 16)
                    if (G, s) == (1, 0):
                        sp.wait_ge(S["hx_ready"], KT // 2)
                        sp.wait_ge(S["hx_pool"], KT // 2)
                        sp.dma_start(fwd[:, :, :], a["fwd"].rearrange("p (t c) -> p t c", t=2)).then_inc(S["tables"], 16)
                        sp.dma_start(inv[:, :, :], a["inv"].rearrange("p (t c) -> p t c", t=4)).then_inc(S["tables"], 16)
                    if (G, s) == (G_Q + 1, 3):
                        sp.wait_ge(S["wg_zero"], 1)
                        for d, (w, b) in enumerate((("gla_wg_f", "gla_bg_f"), ("gla_wg_b", "gla_bg_b"))):
                            sp.dma_start(wg[RANK * d:RANK * d + RANK, d, :], a[w][0]).then_inc(S["wg_in"], 16)
                            sp.dma_start(wg[2 * RANK:NB, d, :], a[b]).then_inc(S["wg_in"], 16)

            for l in range(32):
                load_sub(sp, QC, l, piece(w_out, 2 * (l % 8), 2, 512 * (l // 8), 512), 2, 512)
                if l == 5:
                    sp.wait_ge(S["o_ps"], 4)
                    sp.dma_start(xm[:, :, :], a["x"][0].rearrange("(t p) c -> p t c", p=P)).then_inc(S["x_again"], 16)
                    sp.dma_start(gab[:, :], b_mod[2 * D:3 * D].partition_broadcast(P)).then_inc(S["ga_bias"], 16)

            def up_loads(i, gate=False):
                for s in range(8):
                    if s == 3 and gate:
                        sp.wait_ge(S["gate_used"], i)
                        sp.dma_start(graw[:, :], w_mod[bass.ds(i * P - P, P), 5 * D:6 * D]).then_inc(S["gate_in"], 16)
                    load_sub(sp, QD + i * 2, s, piece(w_up, 4 * (s % 4), 4, i * 256 + FF * (s // 4), 256), 4, 256)

            up_loads(0)
            with sp.Fori(1, NGATE + 1) as i:
                up_loads(i, gate=True)
            with sp.Fori(NGATE + 1, NUP) as i:
                up_loads(i)

            for l in range(88):
                g, s = divmod(l, 22)
                load_sub(sp, QE, l, piece(w_down, 2 * s, 2, 512 * g, 512), 2, 512)
                if l == 1:
                    sp.wait_ge(S["pe_done"], 4 * QE)
                    sp.dma_start(gfb[:, :], b_mod[5 * D:6 * D].partition_broadcast(P)).then_inc(S["gf_bias"], 16)
                    sp.dma_start(gfin[:, :], a["g_final"].partition_broadcast(P)).then_inc(S["gfin_in"], 16)
            for t in range(2):
                sp.wait_ge(S[f"fin{t}"], 1)
                sp.dma_start(out[0, P * t:P * t + P, :], xm[:, t, :]).then_inc(S["out_done"], 16)
            sp.wait_ge(S["out_done"], 32)

        @block.tensor
        def _(pe):
            def ch_sub(q, s, banks, x_hi, x_lo, operand=False, width=256):
                nt = max(1, width // P)
                m = min(P, width)
                r, _ = place(q, s)
                if operand:
                    pe.wait_ge(S["hx_ready"], 2 * (s + 1))
                    pe.wait_ge(S["hx_pool"], 2 * (s + 1))
                hi_in(pe, q, s)
                h = hi[:, r, 0:4 * width].rearrange("p (t c) -> p t c", t=4)
                l = lo[:, r, 0:4 * width].rearrange("p (t c) -> p t c", t=4)
                for k in range(4):
                    for j in range(nt):
                        w = h[:, k, j * P:j * P + m]
                        o = ps[0:m, banks[j], 0:T]
                        pe.matmul(o, w, x_hi[:, 4 * s + k, :], start=(s == 0 and k == 0), stop=False)
                        pe.matmul(o, w, x_lo[:, 4 * s + k, :], start=False, stop=False)
                lo_in(pe, q, s)
                for k in range(4):
                    for j in range(nt):
                        mm = pe.matmul(ps[0:m, banks[j], 0:T], l[:, k, j * P:j * P + m], x_hi[:, 4 * s + k, :],
                                       start=False, stop=(s == 3 and k == 3))
                mm.then_inc(S["pe_done"], 1)

            def tok_sub(q, l, s, last, tiles):
                r, _ = place(q, l)
                hi_in(pe, q, l)
                h = hi[:, r, :].rearrange("p (t c) -> p t c", t=2)
                w = lo[:, r, :].rearrange("p (t c) -> p t c", t=2)
                for k in range(2):
                    for b, th, tl in tiles:
                        pe.matmul(ps[:, b, :], th(2 * s + k), h[:, k, :], start=(s == 0 and k == 0), stop=False)
                        pe.matmul(ps[:, b, :], tl(2 * s + k), h[:, k, :], start=False, stop=False)
                lo_in(pe, q, l)
                for k in range(2):
                    for b, th, tl in tiles:
                        mm = pe.matmul(ps[:, b, :], th(2 * s + k), w[:, k, :], start=False, stop=(s == last and k == 1))
                mm.then_inc(S["pe_done"], 1)

            pe.wait_ge(S["ident_in"], 16)
            pe.wait_ge(S["conds"], 32)
            pe.transpose(ps[:, 3, 0:32], pack[0:32, 0, :], ident(32)).then_inc(S["vt_ps"], 1)

            def turn_vectors(part):
                if part == 0:
                    pe.wait_ge(S["cond_sb"], 1)
                else:
                    pe.wait_ge(S["vt_sb"], part)
                pe.wait_ge(S[("packed", "packed1", "packed2")[part]], (8, 4, 2)[part] * 16)
                for i, n, c0 in (((0, 84, V_C),), ((1, 96, V_BM), (2, 72, V_HC), (3, 99, V_FC), (4, 99, V_FC + 99)),
                                 ((5, 99, 0), (6, 99, 99)))[part]:
                    pe.transpose(ps[:, 3, c0:c0 + n], pack[0:n, i, :], ident(n)).then_inc(S["vt_ps"], 1)

            def filter_hidden(w, x, sem, bank):
                pe.matmul(ps[0:HID, bank, 0:T], w, x, start=True, stop=True).then_inc(sem, 1)

            def filter_out(j):
                if j == 0:
                    pe.wait_ge(S["f2_sb"], 1)
                    pe.wait_ge(S["w3_in"], 16)
                if j >= 4:
                    pe.wait_ge(S["h3_sb"], j - 3)
                t, c = divmod(j, 4)
                pe.matmul(ps[:, 4 + j % 4, :], h2[:, P * t:P * t + P], w3[:, 512 * c:512 * c + 512],
                          start=True, stop=True).then_inc(S["h3_ps"], 1)

            def spectrum(n, t):
                part, j = divmod(n, 4)
                f, c = divmod(j, 2)
                if t == 0:
                    if n == 0:
                        pe.wait_ge(S["fwd_in"], 16)
                        pe.wait_ge(S["h3_sb"], 8)
                    if n >= 4:
                        pe.wait_ge(S["kf_sb"], n - 3)
                    pe.wait_ge(S["sd_done"], part + 1)
                mm = pe.matmul(ps[:, 4 + j, :], fwd_a[:, t, 256 * part + P * f:256 * part + P * f + P],
                               (hsum, hdif)[part][:, t, 512 * c:512 * c + 512], start=(t == 0), stop=(t == 1))
                if t == 1:
                    mm.then_inc(S["kf_ps"], 1)

            def nyquist(c):
                pe.wait_ge(S["kf_sb"], 5 + c)
                for t in range(2):
                    mm = pe.matmul(ps[0:1, 4 + c, :], fwd_a[:, t, 256:257], hsum[:, t, 512 * c:512 * c + 512],
                                   start=(t == 0), stop=(t == 1))
                mm.then_inc(S["kf_ps"], 1)

            def norm_turn(t):
                if t == 0:
                    pe.wait_ge(S["diag_ready"], 4)
                if t < 4:
                    pe.wait_ge(S["kf_sb"], 10 if t < 2 else 5 + t)
                else:
                    pe.wait_ge(S[("xn_act", "xn_dve")[t % 2]], 2 * ((t - 4) // 2 + 1))
                for j in range(4):
                    src = (xtok, ctok)[j // 2]
                    mm = pe.matmul(ps[:, 4 + t % 4, P * j:P * j + P], src[:, j % 2, P * t:P * t + P], diag[:, j, :],
                                   start=True, stop=True)
                mm.then_inc(S["xn_ps"], 1)

            def rows_to_cols(g):
                pe.wait_ge(S["rows_sb"], g + 1)
                if g == 0:
                    pe.wait_ge(S["sel_in"], 16)
                for c in range(4):
                    mm = pe.matmul(ps[:, 2, 2 * (4 * g + c):2 * (4 * g + c) + 2], rows4[:, g % 2, P * c:P * c + P],
                                   sel[:, :], start=True, stop=True)
                mm.then_inc(S["col_ps"], 1)

            for g in range(8):
                for s in range(8):
                    l = 8 * g + s
                    if s == 0:
                        if g == 0:
                            pe.wait_ge(S["cv_ready"], 2)
                        if g >= 2:
                            pe.wait_ge(S["rows_sb"], g - 1)
                    hi_in(pe, QA, l)
                    r, _ = place(QA, l)
                    h = hi[:, r, :].rearrange("p (t c) -> p t c", t=2)
                    lw = lo[:, r, :].rearrange("p (t c) -> p t c", t=2)
                    for k in range(2):
                        pe.matmul(ps[:, g % 2, :], cvec[:, 2 * s + k, :], h[:, k, :], start=(s == 0 and k == 0), stop=False)
                    lo_in(pe, QA, l)
                    for k in range(2):
                        mm = pe.matmul(ps[:, g % 2, :], cvec[:, 2 * s + k, :], lw[:, k, :], start=False,
                                       stop=(s == 7 and k == 1))
                    mm.then_inc(S["pe_done"], 1)
                    if g >= 1 and s == 5:
                        rows_to_cols(g - 1)
                    if l in (2, 21, 25):
                        turn_vectors((2, 21, 25).index(l))
                    if l == 4:
                        pe.wait_ge(S["fload"], 48)
                        filter_hidden(w1[:, :], zf[:, :], S["f1_ps"], 5)
                    if l == 7:
                        pe.wait_ge(S["f1_sb"], 1)
                        filter_hidden(w2[:, :], h1[:, :], S["f2_ps"], 6)
                    if L_OUT <= l < L_OUT + 8:
                        filter_out(l - L_OUT)
                    if L_SPEC <= l < L_SPEC + 16:
                        spectrum(*divmod(l - L_SPEC, 2))
                    if L_NYQ <= l < L_NYQ + 2:
                        nyquist(l - L_NYQ)
                    if L_TURN <= l < L_TURN + KT:
                        norm_turn(l - L_TURN)
            rows_to_cols(7)

            def turn_z(h):
                pe.wait_ge(S["z_done"], h + 1)
                if h == 0:
                    pe.wait_ge(S["xn_act"], KT)
                    pe.wait_ge(S["xn_dve"], KT)
                else:
                    pe.wait_ge(S["y2_done"], 4 * h)
                for t in range(2):
                    for j in range(4):
                        mm = pe.transpose(ps[:, 4 + t, P * j:P * j + P], bv[:, j, P * t:P * t + P], ident())
                    mm.then_inc(S["zt_ps"], 1)

            def dft(h):
                pe.wait_ge(S["zt_sb"], 2 * (h + 1))
                pe.wait_ge(S["tables"], 32)
                if h == 1:
                    pe.wait_ge(S["hrt_done"], 1)
                for f in range(4):
                    for t in range(2):
                        mm = pe.matmul(ps[:, 4 + f, :], fwd[:, t, P * f:P * f + P], zt[:, t, :], start=(t == 0), stop=(t == 1))
                mm.then_inc(S["dft_ps"], 1)

            def dft_back(h):
                pe.wait_ge(S["cplx"], h + 1)
                for j in range(4):
                    for f in range(4):
                        mm = pe.matmul(ps[:, 4 + j // 2, T * (j % 2):T * (j % 2) + T], yf[:, f, P * j:P * j + P],
                                       inv[:, f, :], start=(f == 0), stop=(f == 3))
                mm.then_inc(S["y_ps"], 1)

            def group_mean(h):
                pe.wait_ge(S["hsq_done"], h + 1)
                for j in range(2):
                    mm = pe.matmul(ps[:, 6 + j, :], con[:, K_MEAN, :], sq[:, 2 * j:2 * j + 2, :], start=True, stop=True)
                mm.then_inc(S["hms_ps"], 1)

            def reduce_cols(chunk, bank, c0):
                pe.wait_ge(S["mod_used"], 16 * (chunk + 1))
                for c in range(8):
                    mm = pe.matmul(ps[:, bank, c0 + c:c0 + c + 1], acc[:, chunk % 2, P * c:P * c + P], con[:, K_ONE, 0:1],
                                   start=True, stop=True)
                mm.then_inc(S["red_ps"], 1)

            def gates(j):
                d, t = divmod(j, 4)
                if j == 0:
                    pe.wait_ge(S["rT_ready"], 2)
                    pe.wait_ge(S["rT_one"], 1)
                    pe.wait_ge(S["wg_in"], 64)
                    pe.wait_ge(S["hrt_done"], 2)
                if j >= 3:
                    pe.wait_ge(S["la_done"], j - 2)
                pe.matmul(ps[:, 4 + j % 3, :], rT[:, P * t:P * t + P], wg[:, d, :], start=True, stop=True)\
                    .then_inc(S["la_ps"], 1)

            def pair_sums(p):
                cs = slice(P * p, P * p + P)
                if p == 0:
                    pe.wait_ge(S["la_done"], 8)
                    pe.wait_ge(S["red_sb"], 4)
                    pe.wait_ge(S["kv_act"], 1)
                    pe.wait_ge(S["kv_dve"], 1)
                else:
                    pe.wait_ge(S["g_f32"], p)
                    pe.wait_ge(S["grt_done"], p)
                for d, tri in enumerate((K_TF, K_TB)):
                    for t in range(2):
                        pe.matmul(ps[:, 4, 256 * d + P * t:256 * d + P * t + P], la[:, d, t, cs], con[:, tri, :],
                                  start=True, stop=True)
                for d, tri in enumerate((K_SF, K_SB)):
                    for t in range(2):
                        pe.matmul(ps[:, 5, 256 * d + P * t:256 * d + P * t + P], con[:, tri, :], la[:, d, t, cs],
                                  start=True, stop=True)
                pe.matmul(ps[:, 6, 0:P], con[:, K_SC, :], la[:, 0, 2, cs], start=True, stop=False)
                pe.matmul(ps[:, 6, 0:P], con[:, K_AL, :], la[:, 0, 3, cs], start=False, stop=True)
                pe.matmul(ps[:, 6, P:2 * P], con[:, K_SC, :], la[:, 0, 3, cs], start=True, stop=True)
                pe.matmul(ps[:, 6, 2 * P:3 * P], con[:, K_PC, :], la[:, 1, 2, cs], start=True, stop=True)
                pe.matmul(ps[:, 6, 3 * P:4 * P], con[:, K_PC, :], la[:, 1, 3, cs], start=True, stop=False)
                pe.matmul(ps[:, 6, 3 * P:4 * P], con[:, K_AL, :], la[:, 1, 2, cs], start=False, stop=True)
                for t in range(2):
                    mm = pe.transpose(ps[:, 7, P * t:P * t + P], ktok[:, t, cs], ident())
                mm.then_inc(S["cum_ps"], 1)

            def pair_products(p):
                pe.wait_ge(S["kdc"], 4 * (p + 1))
                pe.wait_ge(S["pairs_in"], 4 * (p + 1))
                if p == 0:
                    pe.wait_ge(S["kv_act"], 3)
                    pe.wait_ge(S["kv_dve"], 3)
                for d in range(2):
                    for hh in range(2):
                        for t in range(2):
                            pe.matmul(ps[64 * hh:64 * hh + 64, 5 + d, 3 * P:4 * P], kc[:, d, t, 64 * hh:64 * hh + 64],
                                      vtok[:, 2 + t, DV * (2 * p + hh):DV * (2 * p + hh) + DV], start=(t == 0), stop=(t == 1))
                for d, c in ((0, 0), (0, 2), (1, 2), (0, 1), (1, 1), (1, 3)):
                    b, slot = u_slot(d, c)
                    r0 = 64 * (c % 2)
                    for hh in range(2):
                        mm = pe.matmul(ps[64 * hh:64 * hh + 64, b, P * slot:P * slot + P],
                                       kd[r0:r0 + 64, d, c // 2, 64 * hh:64 * hh + 64],
                                       vtok[r0:r0 + 64, c // 2, DV * (2 * p + hh):DV * (2 * p + hh) + DV],
                                       start=True, stop=True)
                mm.then_inc(S["u_ps"], 1)
                for hh in range(2):
                    b = 7 if hh == 0 else 4
                    rr = slice(64 * hh, 64 * hh + 64)
                    for t in range(2):
                        for d in range(2):
                            mm = pe.matmul(ps[:, b, P * (2 * t + d):P * (2 * t + d) + P], ke[rr, d, P * t:P * t + P],
                                           qe[rr, d, P * t:P * t + P], start=True, stop=True)
                    mm.then_inc(S["u_ps"], 1)

            def pair_out(p):
                pe.wait_ge(S["sc_set"], 8 * (p + 1))
                pe.wait_ge(S["states"], 8 * (p + 1))
                for hh in range(2):
                    rr = slice(64 * hh, 64 * hh + 64)
                    hcol = slice(DV * (2 * p + hh), DV * (2 * p + hh) + DV)
                    for t in range(2):
                        pe.matmul(ps[:, 5 + hh, P * t:P * t + P], vtok[:, t, hcol], scm[:, hh, t, :], start=True, stop=False)
                        for c in (2 * t, 2 * t + 1):
                            for d in range(2):
                                mm = pe.matmul(ps[:, 5 + hh, CH * c:CH * c + CH], st[rr, d, c, :],
                                               qe[rr, d, CH * c:CH * c + CH], start=False,
                                               stop=(c == 2 * t + 1 and d == 1))
                mm.then_inc(S["o_ps"], 1)

            def pair_mean(p):
                pe.wait_ge(S["gsq_done"], p + 1)
                pe.matmul(ps[:, 7, :], con[:, K_MEAN, :], gsq[:, :, :], start=True, stop=True).then_inc(S["gms_ps"], 1)

            def pair_step(slot):
                p, k = divmod(slot + 1, 5)
                if 0 <= p < 4 and slot > 0:
                    if k == 0:
                        pair_sums(p)
                    if k == 2:
                        pair_products(p)
                    if k == 3:
                        pair_out(p)
                    if k == 4:
                        pair_mean(p)

            for G in range(NGRP):
                q = quad_of(G)
                pair = (2 * (G % 2), 2 * (G % 2) + 1)
                for s in range(subs_of(G)):
                    if s == 0:
                        if G == 0:
                            pe.wait_ge(S["rows_sb"], 8)
                        elif G == 1:
                            pe.wait_ge(S["gx_ready"], 4)
                        elif G <= G_R:
                            pe.wait_ge(S["hy_evac"], 2 * (G - 1))
                        elif G == G_Q:
                            pe.wait_ge(S["hy_evac"], 24)
                        elif G == G_Q + 1:
                            pe.wait_ge(S["rT_ready"], 2)
                        elif G < G_G:
                            if G == G_KV:
                                pe.wait_ge(S["q_evac"], 2)
                            else:
                                pe.wait_ge(S["kv_act"], G - G_KV)
                                pe.wait_ge(S["kv_dve"], G - G_KV)
                        elif G < G_G + 2:
                            pe.wait_ge(S["kv_act"], 3)
                            pe.wait_ge(S["kv_dve"], 3)
                        else:
                            pe.wait_ge(S["g_evac"], G - G_G - 1)
                        if G == 9:
                            reduce_cols(0, pair[0], 256)
                    if G == G_R:
                        pe.wait_ge(S["hc_ready"], KT)
                        hi_in(pe, q, s)
                        r, _ = place(q, s)
                        h = hi[:, r, 0:128].rearrange("p (t c) -> p t c", t=4)
                        lw = lo[:, r, 0:128].rearrange("p (t c) -> p t c", t=4)
                        for k in range(4):
                            for b, th, tl in ((0, hx_hi, hx_lo), (1, hc_hi, hc_lo)):
                                kk = 4 * s + k
                                first = s == 0 and k == 0
                                pe.matmul(ps[0:32, b, 0:T], h[:, k, :], th[:, kk, :], start=first, stop=False,
                                          )
                                pe.matmul(ps[0:32, b, 0:T], h[:, k, :], tl[:, kk, :], start=False, stop=False)
                        lo_in(pe, q, s)
                        for k in range(4):
                            for b, th in ((0, hx_hi), (1, hc_hi)):
                                mm = pe.matmul(ps[0:32, b, 0:T], lw[:, k, :], th[:, 4 * s + k, :], start=False,
                                               stop=(s == 3 and k == 3))
                        mm.then_inc(S["pe_done"], 1)
                    elif G_KV <= G < G_G:
                        def tile_of(x, t):
                            return lambda k: x[:, k, P * t:P * t + P]
                        tok_sub(q, s, s, 7, [(b, tile_of((hx_hi, hc_hi)[b // 2], b % 2), tile_of((hx_lo, hc_lo)[b // 2], b % 2))
                                          for b in range(4)])
                    else:
                        ch_sub(q, s, pair, hx_hi, hx_lo, operand=(G == 0))
                    for h, at5, at3, ay, am in ((0, (5, 0), (5, 3), (6, 3), (8, 0)), (1, (11, 0), (11, 3), (G_R, 3), (G_Q + 1, 0))):
                        if (G, s) == at5:
                            turn_z(h)
                        if (G, s) == at3:
                            dft(h)
                        if (G, s) == ay:
                            dft_back(h)
                        if (G, s) == am:
                            group_mean(h)
                    if G_KV <= G < G_G and s == 1:
                        if G == G_KV:
                            pe.wait_ge(S["hrt_done"], 2)
                        else:
                            pe.wait_ge(S["red_sb"], 1 + G - G_KV)
                        reduce_cols(1 + G - G_KV, 7, 0)
                    if G == G_KV + 1:
                        gates(s)
                    if (G, s) == (G_KV + 2, 5):
                        pair_sums(0)
                    if G >= G_G:
                        pair_step(4 * (G - G_G) + s)

            for g in range(4):
                for s in range(8):
                    if s == 0:
                        if g < 2:
                            pe.wait_ge(S["g_evac"], 3 + g)
                        else:
                            pe.wait_ge(S["wo_evac"], 2 * (g - 1))
                    if g == 0 and s == 0:
                        pe.wait_ge(S["hy_mix"], 2)
                    if g == 0 and s >= 4:
                        pe.wait_ge(S["g_mix"], s - 3)
                    def mix(x, y, t):
                        return lambda k: (x[:, k, P * t:P * t + P] if k < 8 else y[:, k - 8, P * t:P * t + P])
                    b0 = 2 * (g % 2)
                    tok_sub(QC + 2 * g, s, s, 7, [(b0 + t, mix(hm_hi, gm_hi, t), mix(hm_lo, gm_lo, t)) for t in range(2)])
                    if g == 0:
                        pair_step(16 + s)
                    if (g, s) == (0, 6):
                        pe.wait_ge(S["mod_used"], 96)
                        pe.wait_ge(S["grt_done"], 4)
                        pe.wait_ge(S["g_f32"], 4)
                        for c in range(4):
                            mm = pe.matmul(ps[:, 4 + c, :], con[:, K_ONE, :], acc[:, c // 2, 512 * (c % 2):512 * (c % 2) + 512],
                                           start=True, stop=True)
                        mm.then_inc(S["ga_ps"], 1)
            pe.wait_ge(S["ga_ready"], 1)
            pe.wait_ge(S["dg2"], 2)
            for j in range(8):
                if j >= 4:
                    pe.wait_ge(S["h2_f32"], 2 * (j - 3))
                for i in range(2):
                    for t in range(2):
                        k = 2 * j + i
                        mm = pe.matmul(ps[:, 4 + j % 4, 256 * i + P * t:256 * i + P * t + P], xm[:, t, P * k:P * k + P],
                                       dg[:, t, :], start=True, stop=True)
                mm.then_inc(S["xt_ps"], 1)

            pe.wait_ge(S["wo_evac"], 8)

            def up_body(i, first):
                for s in range(8):
                    if first and s < 4:
                        pe.wait_ge(S["h2_ready"], 2 * (s + 1))
                    if s == 0 and not first:
                        pe.wait_ge(S["a_evac"], i * 2)
                    if s == 4 and not first:
                        pe.wait_ge(S["act_f32"], i)
                    g = s // 4
                    r = s % 4
                    q = QD + i * 2
                    hi_in(pe, q, s)
                    h = hi[:, r, :].rearrange("p (t c) -> p t c", t=4)
                    l = lo[:, r, :].rearrange("p (t c) -> p t c", t=4)
                    for k in range(4):
                        for j in range(2):
                            o = ps[:, 2 * g + j, 0:T]
                            pe.matmul(o, h[:, k, j * P:j * P + P], hx_hi[:, 4 * r + k, :], start=(r == 0 and k == 0), stop=False)
                            pe.matmul(o, h[:, k, j * P:j * P + P], hx_lo[:, 4 * r + k, :], start=False, stop=False)
                    lo_in(pe, q, s)
                    for k in range(4):
                        for j in range(2):
                            mm = pe.matmul(ps[:, 2 * g + j, 0:T], l[:, k, j * P:j * P + P], hx_hi[:, 4 * r + k, :],
                                           start=False, stop=(r == 3 and k == 3))
                    mm.then_inc(S["pe_done"], 1)

            up_body(0, True)
            with pe.Fori(1, NGATE + 1) as i:
                up_body(i, False)
            pe.wait_ge(S["gate_used"], NGATE + 1)
            for c in range(4):
                mm = pe.matmul(ps[:, 4 + c, :], con[:, K_ONE, :], gacc[:, 512 * c:512 * c + 512], start=True, stop=True)
            mm.then_inc(S["gf_ps"], 1)
            with pe.Fori(NGATE + 1, NUP) as i:
                up_body(i, False)

            def act_of(x, t):
                return lambda k: x[:, k, P * t:P * t + P]

            for g in range(4):
                for s in range(22):
                    if s == 0:
                        if g == 0:
                            pe.wait_ge(S["a_evac"], 2 * NUP)
                            pe.wait_ge(S["act_ready"], NUP - 1)
                        if g == 1:
                            pe.wait_ge(S["act_f32"], NUP)
                        if g >= 2:
                            pe.wait_ge(S["dn_evac"], 2 * (g - 1))
                    if g == 0 and s == 21:
                        pe.wait_ge(S["act_ready"], NUP)
                    b0 = 2 * (g % 2)
                    tok_sub(QE, 22 * g + s, s, 21, [(b0 + t, act_of(act_hi, t), act_of(act_lo, t)) for t in range(2)])

        PROD = {6: 0, 10: 1, 14: 2, 20: 3}

        @block.scalar
        def _(act):
            def f(o, i, fn, sem, **kw):
                act.activation(o, i, fn, **kw).then_inc(S[sem], 1)

            act.wait_ge(S["cond_sb"], 1)
            f(sc[:, :, :], vec[:, 0:32].rearrange("p (a b) -> p a b", a=2), ACT.Silu, "sc_done")
            act.wait_ge(S["sc_done"], 1)
            act.wait_ge(S["cv_zero"], 1)
            for j in range(2):
                f(cvec[:, :, 2 * j], sc[:, j, :], ACT.Copy, "cv_hi")

            def turn_evac(t):
                act.wait_ge(S["xn_ps"], t + 1)
                f(xn[:, t, :], ps[:, 4 + t % 4, 0:T], ACT.Copy, "xn_act")
                f(cn[:, t, :], ps[:, 4 + t % 4, T:2 * T], ACT.Copy, "xn_act")

            def square_in(j):
                act.wait_ge(S[("x_in0", "x_in1", "ctx_in0", "ctx_in1")[j]], 16)
                if j:
                    act.wait_ge(S["sq_done"], j)
                act.activation(junk[:, :], (xtok, ctok)[j // 2][:, j % 2, :], ACT.Square, accum_out=ss[:, j:j + 1])\
                    .then_inc(S["sq_done"], 1)

            for l in range(64):
                round_sub(act, QA, l)
                if l == 6:
                    act.wait_ge(S["f1_arg"], 1)
                    f(h1[:, :], sr[:, :], ACT.Sin, "f1_sb")
                if l == 9:
                    act.wait_ge(S["f2_arg"], 1)
                    f(h2[:, :], sr[:, :], ACT.Sin, "f2_sb")
                if l in (28, 31, 34, 37):
                    square_in((l - 28) // 3)
                if l == 38:
                    act.wait_ge(S["sq_done"], 4)
                    act.wait_ge(S["epsok"], 1)
                    f(rs[:, 0:4], ss[:, 0:4], ACT.Sqrt, "rstd_done", scale=1.0 / D, bias=eps[:, 0:1])
                n, odd = divmod(l - LAG - L_SPEC, 2)
                if odd and 0 <= n < 8:
                    part, j = divmod(n, 4)
                    act.wait_ge(S["kf_ps"], n + 1)
                    f((kre, kim)[part][:, j // 2, 512 * (j % 2):512 * (j % 2) + 512], ps[:, 4 + j, :], ACT.Copy, "kf_sb")
                c = l - LAG - L_NYQ
                if 0 <= c < 2:
                    act.wait_ge(S["kf_ps"], 9 + c)
                    act.wait_ge(S["kf_sb"], 8)
                    f(kim[0:1, 0, 512 * c:512 * c + 512], ps[0:1, 4 + c, :], ACT.Copy, "kf_sb")
                t = l - LAG - L_TURN
                if 0 <= t < KT and t % 2 == 0:
                    turn_evac(t)

            def operand_hi(t, src, dst, j, sem):
                f(dst[:, t, :], src[:, t, :], ACT.Identity, sem, scale=gx[:, j, t:t + 1], bias=mcol[:, j, t:t + 1])

            def hy_mid(G):
                half, col, jg = HY[G]
                dst = {C_V: bv, C_X1: bx1, C_X0: bx0}[col]
                if half == 0:
                    act.wait_ge(S["hx_ready"], KT // 2)
                    act.wait_ge(S["hx_pool"], KT // 2)
                    if col == C_X0:
                        act.wait_ge(S["hc_ready"], KT)
                elif col == C_X1:
                    act.wait_ge(S["z_done"], 1)
                elif col == C_V:
                    act.wait_ge(S["hy_mix"], 1)
                else:
                    act.wait_ge(S["y3_done"], 1)
                act.wait_ge(S["pe_done"], 4 * (quad_of(G) + 1))
                for jj in range(2):
                    tile = col // P + 4 * half + 2 * jg + jj
                    f(dst[:, 2 * jg + jj, :], ps[:, 2 * (G % 2) + jj, 0:T], ACT.Copy, "mid_tap",
                      scale=vec[:, V_HC + 24 + tile:V_HC + 25 + tile])

            def hyena(h, step):
                if step == 0:
                    for t in range(2):
                        act.wait_ge(S["zt_ps"], 2 * h + t + 1)
                        if h == 1:
                            act.wait_ge(S["dft_ps"], 1)
                        f(zt[:, t, :], ps[:, 4 + t, :], ACT.Copy, "zt_sb")
                if step == 1:
                    act.wait_ge(S["y3_done"], h + 1)
                    f(sq[:, :, :], bv[:, :, :], ACT.Square, "hsq_done")
                if step == 2:
                    act.wait_ge(S["hms_ps"], h + 1)
                    f(rt[:, :, :], ps[:, 6:8, :].rearrange("p b (j c) -> p (b j) c", j=2), ACT.Ln, "hln", bias=eps[:, 0:1])
                    act.wait_ge(S["hln"], h + 1)
                    f(rt[:, :, :], rt[:, :, :], ACT.Exp, "hrt_done", scale=-0.5)
                if step == 3:
                    act.wait_ge(S["hy_f32"], 4 * (h + 1))
                    f(hm_hi[:, 4 * h:4 * h + 4, :], bv[:, :, :], ACT.Copy, "hy_hi")

            def kv_evac(G):
                act.wait_ge(S["pe_done"], 4 * quad_of(G) + 8)
                if G == G_KV:
                    act.wait_ge(S["cplx"], 2)
                else:
                    act.wait_ge(S["hy_mix"], 2)
                for b in range(2):
                    dst = ktok[:, b, :] if G == G_KV else vtok[:, b, 512 * (G - G_KV - 1):512 * (G - G_KV)]
                    ins = act.activation(dst, ps[:, b, :], ACT.Copy)
                ins.then_inc(S["kv_act"], 1)

            def softplus(j):
                act.wait_ge(S["la_ps"], j + 1)
                if j:
                    act.wait_ge(S["la_done"], j)
                f(ea[:, :], ps[:, 4 + j % 3, :], ACT.Abs, "act_own")
                act.wait_ge(S["act_own"], 2 * j + 1)
                f(ea[:, :], ea[:, :], ACT.Exp, "act_own", scale=-1.0)
                act.wait_ge(S["act_own"], 2 * j + 2)
                f(ea[:, :], ea[:, :], ACT.Ln, "la_exp", bias=1.0)

            def gla(slot):
                p, k = divmod(slot, 5)
                if k == 0 and p < 4:
                    act.wait_ge(S["cum_ps"], p + 1)
                    flat = "p a b -> p (a b)"
                    f(ep[:, :, :].rearrange(flat), ps[:, 4, :], ACT.Exp, "exps")
                    f(ke[:, :, :].rearrange(flat), ps[:, 4, :], ACT.Exp, "exps", scale=-1.0)
                    f(kd[:, :, :, :].rearrange("p a b c -> p (a b c)"), ps[:, 5, :], ACT.Exp, "exps")
                    f(kc[:, :, :, :].rearrange("p a b c -> p (a b c)"), ps[:, 6, :], ACT.Exp, "exps")
                if k == 3 and p < 4:
                    act.wait_ge(S["o_ps"], p + 1)
                    f(gsq[:, :, :], ps[:, 5:7, 0:T], ACT.Square, "gsq_done")
                if k == 4 and p < 4:
                    act.wait_ge(S["gms_ps"], p + 1)
                    f(grt[:, :, :].rearrange("p a b -> p (a b)"), ps[:, 7, :], ACT.Ln, "gln", bias=eps[:, 0:1])
                    act.wait_ge(S["gln"], p + 1)
                    f(grt[:, :, :], grt[:, :, :], ACT.Exp, "grt_done", scale=-0.5)
                if slot % 4 == 2 and slot >= 6 and (slot - 6) // 4 < 4:
                    g = (slot - 6) // 4
                    act.wait_ge(S["pe_done"], 4 * (quad_of(G_G + g) + 1))
                    if g == 3:
                        act.wait_ge(S["g_mix"], 1)
                    z = (2 * g + 2) % 8
                    f(sg[:, z:z + 2, :], ps[:, 2 * (g % 2):2 * (g % 2) + 2, 0:T], ACT.Silu, "g_evac")
                if slot - 1 in PROD:
                    p = PROD[slot - 1]
                    act.wait_ge(S["g_prod"], p + 1)
                    f(gm_hi[:, 2 * p:2 * p + 2, :], sg[:, 2 * p:2 * p + 2, :], ACT.Copy, "g_hi")

            HYS = {(5, 2): (0, 0), (7, 3): (0, 1), (8, 1): (0, 2), (8, 3): (0, 3),
                   (11, 2): (1, 0), (G_Q + 1, 0): (1, 1), (G_Q + 1, 1): (1, 2), (G_Q + 1, 3): (1, 3)}
            for s in range(4):
                round_sub(act, QB, s)
            act.wait_ge(S["vt_sb"], 3)
            act.wait_ge(S["gx_ready"], 4)
            act.wait_ge(S["xn_dve"], KT)
            act.wait_ge(S["xn_act"], KT)
            for t in range(KT):
                operand_hi(t, xn, hx_hi, 0, "hx_hi_ready")
            for G in range(NGRP):
                for s in range(subs_of(G)):
                    if G > 0:
                        round_sub(act, quad_of(G), s, 128 if G == G_R else 1024)
                    if 1 <= G < 5:
                        operand_hi(4 * G - 4 + s, cn, hc_hi, 1, "hc_hi_ready")
                    if 1 <= G <= G_R and s == 2:
                        hy_mid(G - 1)
                    if (G, s) in HYS:
                        hyena(*HYS[G, s])
                    if G_KV < G <= G_G and s == 0:
                        kv_evac(G - 1)
                    if G == G_KV + 1 and s >= 1:
                        softplus(s - 1)
                    if (G, s) == (G_KV + 2, 0):
                        softplus(7)
                    if (G, s) == (G_KV + 2, 7):
                        gla(0)
                    if G >= G_G and (G, s) != (G_G, 0):
                        gla(4 * (G - G_G) + s)

            def ssq(g):
                for t in range(2):
                    act.wait_ge(S["xm_done"], 2 * g + t + 1)
                    if g + t:
                        act.wait_ge(S["ssm"], 2 * g + t)
                    act.activation(sqj[:, :], xm[:, t, 512 * g:512 * g + 512], ACT.Square,
                                   accum_out=ss[:, 4 * t + g:4 * t + g + 1]).then_inc(S["ssm"], 1)

            for g in range(4):
                for s in range(8):
                    round_sub(act, QC + 2 * g, s)
                    if g == 0:
                        gla(16 + s)
                    if g >= 1 and s == 3:
                        ssq(g - 1)
            for s in range(4):
                round_sub(act, QD, s)
            ssq(3)
            act.wait_ge(S["rsum"], 1)
            f(rs[:, 0:2], rs[:, 0:2], ACT.Sqrt, "rstd2", scale=1.0 / D, bias=eps[:, 0:1])
            for j in range(8):
                act.wait_ge(S["h2_f32"], 2 * j + 2)
                f(hx_hi[:, 2 * j:2 * j + 2, :], h2f[:, j % 2, :, :], ACT.Copy, "h2_hi")

            def silu_of(i):
                act.wait_ge(S["conv_done"], i + 1)
                f(cv[:, :, :], cv[:, :, :], ACT.Silu, "silu_done")

            def act_hi_of(i):
                act.wait_ge(S["act_f32"], i + 1)
                f(act_hi[:, bass.ds(i * 2, 2), :], a32[:, :, :], ACT.Copy, "act_h")

            def up_body(i, first):
                q = QD + i * 2
                for s in range(4 if first else 0, 8):
                    if s == 7:
                        act.wait_ge(S["pe_done"], q * 4 + 4)
                        if not first:
                            act.wait_ge(S["conv_done"], i)
                        for j in range(2):
                            f(ap[:, j, :, 1:65], ps[:, j, 0:T].rearrange("p (y x) -> p y x", y=4), ACT.Copy, "a_evac")
                    round_sub(act, q, s)
                    if s == 0 and not first:
                        silu_of(i - 1)
                    if s == 3 and not first:
                        act_hi_of(i - 1)

            act.wait_ge(S["ap_zero"], 1)
            up_body(0, True)
            with act.Fori(1, NUP) as i:
                up_body(i, False)
            silu_of(NUP - 1)
            act_hi_of(NUP - 1)

            def ssq_e(g):
                for t in range(2):
                    act.wait_ge(S["dn_sum"], 2 * g + t + 1)
                    if g + t:
                        act.wait_ge(S["ssf"], 2 * g + t)
                    act.activation(ssj[:, :], xm[:, t, 512 * g:512 * g + 512], ACT.Square,
                                   accum_out=ss3[:, 4 * t + g:4 * t + g + 1]).then_inc(S["ssf"], 1)

            for l in range(88):
                if l == 0:
                    act.wait_ge(S["gf_ps"], 1)
                round_sub(act, QE, l)
                if l in (24, 46):
                    g = l // 22 - 1
                    act.wait_ge(S["pe_done"], 4 * QE + 22 * (g + 1))
                    if g == 0:
                        act.wait_ge(S["act_ready"], NUP)
                    for t in range(2):
                        f(dr[:, g, t, :], ps[:, 2 * g + t, :], ACT.Copy, "dn_evac")
                if l in (48, 54, 72):
                    ssq_e({48: 0, 54: 1, 72: 2}[l])
            ssq_e(3)
            act.wait_ge(S["rsum"], 2)
            f(rs[:, 2:4], rs[:, 2:4], ACT.Sqrt, "rstd3", scale=1.0 / D, bias=eps[:, 0:1])
            act.wait_ge(S["rinv"], 1)
            f(xm[:, 0, :], xm[:, 0, :], ACT.Copy, "fin0", scale=rs[:, 2:3])

        @block.vector
        def _(dve):
            own = Own(dve, S["dve_own"])

            def sg_(ins, sem):
                ins.then_inc(S[sem], 1)

            def mod_unit(m):
                c, k = divmod(m, 16)
                src = mraw[:, m % 2, :]
                dst = acc[:, c % 2, :]
                dve.wait_ge(MOD[m % 2], 16 * (m // 2 + 1))
                if k == 0:
                    if 2 <= c < 6:
                        dve.wait_ge(S["red_ps"], c - 1)
                    sg_(dve.tensor_scalar(dst, src, sc[:, 0, k:k + 1], None, ALU.mult), "mod_used")
                else:
                    dve.wait_ge(S["mod_used"], m)
                    sg_(dve.scalar_tensor_tensor(dst, src, sc[:, 0, k:k + 1], dst, ALU.mult, ALU.add), "mod_used")

            sg_(dve.memset(eps[:, :], EPS), "epsok")
            dve.wait_ge(S["vt_ps"], 1)
            sg_(dve.tensor_copy(vec[:, 0:32], ps[:, 3, 0:32]), "cond_sb")
            dve.wait_ge(S["cv_hi"], 2)
            for j in range(2):
                sg_(dve.tensor_tensor(cvec[:, :, 2 * j + 1], sc[:, j, :], cvec[:, :, 2 * j].bitcast(F32), ALU.subtract),
                    "cv_ready")

            def sine_arg(src, b, sem):
                own(dve.tensor_scalar(sa[:, :], src, vec[0:HID, b:b + 1], vec[0:HID, V_FR:V_FR + 1], ALU.add, ALU.mult))
                own.wait()
                own(dve.tensor_scalar(sk[:, :], sa[:, :], 1.0 / (2 * np.pi), 12582912.0, ALU.mult, ALU.add))
                own.wait()
                own(dve.tensor_scalar(sk[:, :], sk[:, :], 12582912.0, None, ALU.subtract))
                own.wait()
                own(dve.scalar_tensor_tensor(sr[:, :], sk[:, :], -6.28125, sa[:, :], ALU.mult, ALU.add))
                own.wait()
                own(dve.scalar_tensor_tensor(sr[:, :], sk[:, :], 6.28125 - 2 * np.pi, sr[:, :], ALU.mult, ALU.add))
                own.wait()
                sg_(dve.tensor_scalar(sr[:, :], sr[:, :], 3.1415925, -3.1415925, ALU.min, ALU.max), sem)

            def turn_evac(t):
                dve.wait_ge(S["xn_ps"], t + 1)
                sg_(dve.tensor_copy(xn[:, t, :], ps[:, 4 + t % 4, 0:T]), "xn_dve")
                sg_(dve.tensor_copy(cn[:, t, :], ps[:, 4 + t % 4, T:2 * T]), "xn_dve")

            def rows_out(g):
                dve.wait_ge(S["pe_done"], 8 * (g + 1))
                if g >= 2:
                    dve.wait_ge(S["col_ps"], g - 1)
                sg_(dve.tensor_copy(rows4[:, g % 2, :], ps[0:4, g % 2, :]), "rows_sb")

            def tap(j):
                t, c = divmod(j, 4)
                if j == 0:
                    dve.wait_ge(S["decay_in"], 16)
                dve.wait_ge(S["h3_ps"], j + 1)
                sg_(dve.tensor_tensor(taps[:, t, 512 * c:512 * c + 512], ps[:, 4 + j % 4, :],
                                      decay[:, t, 512 * (c % 2):512 * (c % 2) + 512], ALU.mult), "h3_sb")

            for l in range(64):
                if l % 4 != 3:
                    rest_sub(dve, QA, l)
                if l == 3:
                    dve.wait_ge(S["vt_ps"], 2)
                    sg_(dve.tensor_copy(vec[:, 32:84], ps[:, 3, 32:84]), "vt_sb")
                if l == 5:
                    dve.wait_ge(S["vt_sb"], 1)
                    dve.wait_ge(S["f1_ps"], 1)
                    sine_arg(ps[0:HID, 5, 0:T], V_B1, "f1_arg")
                if l == 8:
                    dve.wait_ge(S["f2_ps"], 1)
                    dve.wait_ge(S["f1_sb"], 1)
                    sine_arg(ps[0:HID, 6, 0:T], V_B2, "f2_arg")
                if 0 <= l - L_OUT - LAG < 8:
                    tap(l - L_OUT - LAG)
                if l == L_OUT + LAG + 8:
                    dve.wait_ge(S["h3_sb"], 8)
                    dve.wait_ge(S["row0"], 2)
                    sg_(dve.tensor_tensor(hsum[:, :, :], taps[:, :, 0:HYW], taps[:, :, HYW:2 * HYW], ALU.add), "sd_done")
                if l == L_OUT + LAG + 10:
                    sg_(dve.tensor_tensor(hdif[:, :, :], taps[:, :, 0:HYW], taps[:, :, HYW:2 * HYW], ALU.subtract), "sd_done")
                if l == 24:
                    dve.wait_ge(S["vt_ps"], 6)
                    sg_(dve.tensor_copy(vec[:, 84:450], ps[:, 3, 84:450]), "vt_sb")
                if l == 28:
                    dve.wait_ge(S["vt_ps"], 8)
                    sg_(dve.tensor_copy(vec[:, 450:NV], ps[:, 3, 0:NV - 450]), "vt_sb")
                if l % 8 == 2 and l > 8:
                    rows_out(l // 8 - 1)
                if l == 40:
                    dve.wait_ge(S["rstd_done"], 1)
                    own(dve.reciprocal(rs[:, 0:4], rs[:, 0:4]))
                    own.wait()
                    for j in range(4):
                        sg_(dve.tensor_scalar(diag[:, j, :], ident(), rs[:, j:j + 1], None, ALU.mult), "diag_ready")
                t = l - LAG - L_TURN
                if 0 <= t < KT and t % 2:
                    turn_evac(t)
            for s in range(3):
                rest_sub(dve, QB, s)
            rows_out(7)
            dve.wait_ge(S["col_ps"], 8)
            dve.wait_ge(S["vt_sb"], 3)
            for j in range(2):
                sg_(dve.tensor_tensor(mcol[:, j, :], ps[:, 2, j:64:2], vec[:, V_BM:V_BM + 32], ALU.add), "gx_ready")
            dve.wait_ge(S["gx_ready"], 2)
            for j in range(2):
                sg_(dve.scalar_tensor_tensor(gx[:, j, :], mcol[:, j, 16:32], 1.0, vec[:, V_GA:V_GA + 16], ALU.add, ALU.mult),
                    "gx_ready")
            dve.wait_ge(S["gx_ready"], 4)
            dve.wait_ge(S["xn_act"], KT)

            def operand_lo(t, src, dst, dst_hi, j, hi_sem, sem):
                b = 2 * j + t % 2
                if j == 0 and t >= 2:
                    dve.wait_ge(S[("hx_ready", "hx_pool")[t % 2]], t // 2)
                if j == 1 and t >= 2:
                    dve.wait_ge(S[sem], t - 1)
                ins = dve.tensor_scalar(hf[:, b, :], src[:, t, :], gx[:, j, t:t + 1], mcol[:, j, t:t + 1], ALU.mult, ALU.add)
                if j == 0 and t % 2:
                    sg_(ins, "hx_f32")
                    return
                own(ins)
                own.wait()
                dve.wait_ge(S[hi_sem], t + 1)
                sg_(dve.tensor_tensor(dst[:, t, :], hf[:, b, :], dst_hi[:, t, :].bitcast(F32), ALU.subtract), sem)

            def hy_sides(G):
                half, col, jg = HY[G]
                dst = {C_V: bv, C_X1: bx1, C_X0: bx0}[col]
                dve.wait_ge(S["mid_tap"], 2 * G + 2)
                if G == 9:
                    dve.wait_ge(S["red_ps"], 1)
                    sg_(dve.tensor_tensor(m2[:, 0:8], ps[:, 2, 256:264], vec[:, V_BM + 48:V_BM + 56], ALU.add), "red_sb")
                for jj in range(2):
                    o, src = dst[:, 2 * jg + jj, :], ps[:, 2 * (G % 2) + jj, :]
                    w = V_HC + col // P + 4 * half + 2 * jg + jj
                    own(dve.scalar_tensor_tensor(o[:, 1:T], src[:, 0:T - 1], vec[:, w:w + 1], o[:, 1:T], ALU.mult, ALU.add))
                for jj in range(2):
                    o, src = dst[:, 2 * jg + jj, :], ps[:, 2 * (G % 2) + jj, :]
                    w = V_HC + 48 + col // P + 4 * half + 2 * jg + jj
                    own.wait(1 - jj if jj == 0 else 0)
                    sg_(dve.scalar_tensor_tensor(o[:, 0:T - 1], src[:, 1:T], vec[:, w:w + 1], o[:, 0:T - 1], ALU.mult, ALU.add),
                        "hy_evac")

            def spectra_product(h):
                cs = slice(512 * h, 512 * h + 512)
                dve.wait_ge(S["dft_ps"], h + 1)
                t0, t1 = tt[:, 0, :], tt[:, 1, :]
                for f in range(2):
                    re, im = ps[:, 4 + f, :], ps[:, 6 + f, :]
                    own(dve.tensor_tensor(t0, re, kre[:, f, cs], ALU.mult))
                    own(dve.tensor_tensor(t1, im, kim[:, f, cs], ALU.mult))
                    own(dve.tensor_tensor(yf[:, 2 + f, :], re, kim[:, f, cs], ALU.mult))
                    own.wait(1)
                    own(dve.tensor_tensor(yf[:, f, :], t0, t1, ALU.subtract))
                    own.wait()
                    if f == 0:
                        own(dve.tensor_copy(yf[0:1, 0, :], t0[0:1, :]))
                        own.wait()
                    own(dve.tensor_tensor(t0, im, kre[:, f, cs], ALU.mult))
                    own.wait()
                    if f == 0:
                        own(dve.tensor_tensor(yf[:, 2, :], yf[:, 2, :], t0, ALU.add))
                        own.wait()
                        own(dve.tensor_copy(yf[0:1, 2, :], t1[0:1, :]))
                        own.wait()
                    else:
                        sg_(dve.tensor_tensor(yf[:, 3, :], yf[:, 3, :], t0, ALU.add), "cplx")

            def hyena(h, step):
                if step == 0:
                    spectra_product(h)
                if step == 1:
                    dve.wait_ge(S["y_ps"], h + 1)
                    for j in range(4):
                        sg_(dve.scalar_tensor_tensor(bv[:, j, :], bv[:, j, :], vec[:, V_HB + 4 * h + j:V_HB + 4 * h + j + 1],
                                                     ps[:, 4 + j // 2, T * (j % 2):T * (j % 2) + T], ALU.mult, ALU.add), "y2_done")
                if step == 2:
                    dve.wait_ge(S["hrt_done"], h + 1)
                    for j in range(4):
                        sg_(dve.scalar_tensor_tensor(bv[:, j, :], bv[:, j, :], vec[:, V_HG + 4 * h + j:V_HG + 4 * h + j + 1],
                                                     rt[:, j, :], ALU.mult, ALU.mult), "hy_f32")

            def kv_evac(G):
                dve.wait_ge(S["pe_done"], 4 * quad_of(G) + 8)
                if G > G_KV:
                    dve.wait_ge(S["hy_mix"], 2)
                for b in (2, 3):
                    dst = ktok[:, b, :] if G == G_KV else vtok[:, b, 512 * (G - G_KV - 1):512 * (G - G_KV)]
                    ins = dve.tensor_copy(dst, ps[:, b, :])
                sg_(ins, "kv_dve")

            def red_out(c):
                dve.wait_ge(S["red_ps"], c + 1)
                sg_(dve.tensor_tensor(m2[:, 8 * c:8 * c + 8], ps[:, 7, 0:8], vec[:, V_BM + 48 + 8 * c:V_BM + 56 + 8 * c], ALU.add),
                    "red_sb")

            def log_gate(j):
                d, t = divmod(j, 4)
                dve.wait_ge(S["la_exp"], j + 1)
                sg_(dve.scalar_tensor_tensor(la[:, d, t, :], ps[:, 4 + j % 3, :], 0.0, ea[:, :], ALU.min, ALU.subtract), "la_done")

            def pair_in(p):
                dve.wait_ge(S["exps"], 4 * p + 4)
                for d in range(2):
                    sg_(dve.tensor_tensor(qe[:, d, :], qt[:, p, :], ep[:, d, :], ALU.mult), "pairs_in")
                for d in range(2):
                    sg_(dve.tensor_tensor(ke[:, d, :], ke[:, d, :], ps[:, 7, 0:T], ALU.mult), "pairs_in")

            def pair_mid(p):
                dve.wait_ge(S["u_ps"], 3 * p + 1)
                sg_(dve.tensor_copy(st[:, 0, 0, :], ps[:, 5, 3 * P:4 * P]), "states")
                sg_(dve.tensor_copy(st[:, 1, 3, :], ps[:, 6, 3 * P:4 * P]), "states")
                for k in range(3):
                    for d, c, nxt, e in ((0, k, k + 1, CH * k + CH - 1), (1, 3 - k, 2 - k, CH * (3 - k))):
                        b, slot = u_slot(d, c)
                        dve.wait_ge(S["states"], 8 * p + 2 * k + d + 1)
                        sg_(dve.scalar_tensor_tensor(st[:, d, nxt, :], st[:, d, c, :], ep[:, d, e:e + 1],
                                                     ps[:, b, P * slot:P * slot + P], ALU.mult, ALU.add), "states")
                n = 8 * p
                for hh in range(2):
                    dve.wait_ge(S["u_ps"], 3 * p + 2 + hh)
                    b = 7 if hh == 0 else 4
                    v = ps[:, b, :].rearrange("p (t d i) -> p t d i", t=2, d=2)
                    for k in (0, 1):
                        r = slice(CH * k, CH * k + CH)
                        sg_(dve.tensor_copy(scm[r, hh, :, r], v[r, :, 1, r]), "sc_set")
                    for k in (0, 1):
                        r = slice(CH * k, CH * k + CH)
                        n += 1
                        dve.wait_ge(S["sc_set"], n + k * 1)
                        sg_(dve.copy_predicated(scm[r, hh, :, r], mask[r, :, :], v[r, :, 0, r]), "sc_set")
                    n += 2

            def pair_norm(p):
                dve.wait_ge(S["grt_done"], p + 1)
                sg_(dve.scalar_tensor_tensor(sg[:, 2 * p:2 * p + 2, :], ps[:, 5:7, 0:T], vec[:, V_GG:V_GG + 1], grt[:, :, :],
                                             ALU.mult, ALU.mult), "g_f32")

            def gla(slot):
                p, k = divmod(slot, 5)
                if p < 4:
                    if k == 0:
                        pair_in(p)
                    if k == 2:
                        pair_mid(p)
                    if k == 4:
                        pair_norm(p)
                if slot in PROD:
                    p = PROD[slot]
                    z = (2 * p + 2) % 8
                    dve.wait_ge(S["g_evac"], p + 1)
                    dve.wait_ge(S["g_f32"], p + 1)
                    sg_(dve.tensor_tensor(sg[:, 2 * p:2 * p + 2, :], sg[:, 2 * p:2 * p + 2, :], sg[:, z:z + 2, :], ALU.mult),
                        "g_prod")

            HYS = {(6, 1): (0, 0), (7, 1): (0, 1), (8, 2): (0, 2), (G_R, 1): (1, 0), (G_Q, 1): (1, 1), (G_Q + 1, 2): (1, 2)}
            for G in range(NGRP):
                for s in range(subs_of(G)):
                    if G == 0:
                        for t in range(4 * s, 4 * s + 4):
                            operand_lo(t, xn, hx_lo, hx_hi, 0, "hx_hi_ready", "hx_ready")
                    if s % 4 != 3 and G > 0:
                        rest_sub(dve, quad_of(G), s, 128 if G == G_R else 1024)
                    if 1 <= G < 5:
                        operand_lo(4 * G - 4 + s, cn, hc_lo, hc_hi, 1, "hc_hi_ready", "hc_ready")
                    if 1 <= G <= G_R and s == 2:
                        hy_sides(G - 1)
                    if (G, s) in HYS:
                        hyena(*HYS[G, s])
                    if (G, s) == (G_Q, 2):
                        dve.wait_ge(S["pe_done"], 4 * (quad_of(G_R) + 1))
                        for b in range(2):
                            sg_(dve.tensor_copy(rT[0:32, T * b:T * b + T], ps[0:32, b, 0:T]), "rT_ready")
                    if (G, s) in ((G_Q + 1, 2), (G_Q + 2, 0)):
                        j = G - G_Q - 1
                        dve.wait_ge(S["pe_done"], 4 * (quad_of(G_Q + j) + 1))
                        b = 2 * ((G_Q + j) % 2)
                        sg_(dve.tensor_scalar(qt[:, 2 * j:2 * j + 2, :], ps[:, b:b + 2, 0:T], DK ** -0.5, None, ALU.mult), "q_evac")
                    if G_KV < G <= G_G and s == 0:
                        kv_evac(G - 1)
                    if (G, s) == (G_G, 0):
                        sg_(dve.memset(scm[:, :, :, :], 0.0), "scm_zero")
                        dve.wait_ge(S["scm_zero"], 1)
                    for m in MODS[G, s]:
                        mod_unit(m)
                    if G_KV <= G < G_G and s == 3:
                        red_out(1 + G - G_KV)
                    if (G, s) == (G_KV + 2, 3):
                        dve.wait_ge(S["red_sb"], 4)
                        own(dve.scalar_tensor_tensor(g2[:, :], m2[:, 16:32], 1.0, vec[:, V_GF:V_GF + 16], ALU.add, ALU.mult))
                    if G == G_KV + 1 and s >= 1:
                        log_gate(s - 1)
                    if (G, s) == (G_KV + 2, 0):
                        log_gate(7)
                    if G >= G_G:
                        gla(4 * (G - G_G) + s)

            def residual(g, gate, src, tmp, evac, done, get):
                cs = slice(512 * g, 512 * g + 512)
                for t in range(2):
                    sg_(dve.tensor_tensor(tmp[:, t, :], src(t), gate[:, cs], ALU.mult), evac)
                for t in range(2):
                    dve.wait_ge(S[evac], get + 1 + t)
                    sg_(dve.tensor_tensor(xm[:, t, cs], xm[:, t, cs], tmp[:, t, :], ALU.add), done)

            def wo_out(g):
                dve.wait_ge(S["pe_done"], 4 * QC + 8 * (g + 1))
                dve.wait_ge(S["x_again"], 16)
                dve.wait_ge(S["ga_ready"], 1)
                residual(g, gab, lambda t: ps[:, 2 * (g % 2) + t, :], wt, "wo_evac", "xm_done", 2 * g)

            for g in range(4):
                for s in range(8):
                    if s % 4 != 3:
                        rest_sub(dve, QC + 2 * g, s)
                    if g == 0:
                        gla(16 + s)
                    if (g, s) == (0, 7):
                        dve.wait_ge(S["ga_ps"], 1)
                        dve.wait_ge(S["ga_bias"], 16)
                        sg_(dve.tensor_tensor(gab[:, :], ps[:, 4:8, :].rearrange("p a b -> p (a b)"), gab[:, :], ALU.add), "ga_ready")
                    if g >= 1 and s == 2:
                        wo_out(g - 1)
            for s in range(3):
                rest_sub(dve, QD, s)
            wo_out(3)
            dve.wait_ge(S["ssm"], 8)
            sg_(dve.tensor_reduce(rs[:, 0:2], ss[:, :].rearrange("p (t g) -> p t g", t=2), AXX, ALU.add), "rsum")
            dve.wait_ge(S["rstd2"], 1)
            own(dve.reciprocal(rs[:, 0:2], rs[:, 0:2]))
            own.wait()
            for t in range(2):
                sg_(dve.tensor_scalar(dg[:, t, :], ident(), rs[:, t:t + 1], None, ALU.mult), "dg2")

            def h2_lo(j):
                dve.wait_ge(S["h2_hi"], j + 1)
                sg_(dve.tensor_tensor(hx_lo[:, 2 * j:2 * j + 2, :], h2f[:, j % 2, :, :],
                                      hx_hi[:, 2 * j:2 * j + 2, :].bitcast(F32), ALU.subtract), "h2_ready")

            for j in range(8):
                dve.wait_ge(S["xt_ps"], j + 1)
                if j >= 2:
                    dve.wait_ge(S["h2_ready"], j - 1)
                for i in range(2):
                    k = 2 * j + i
                    sg_(dve.tensor_scalar(h2f[:, j % 2, i, :], ps[:, 4 + j % 4, T * i:T * i + T], g2[:, k:k + 1],
                                          m2[:, k:k + 1], ALU.mult, ALU.add), "h2_f32")
                if j:
                    h2_lo(j - 1)
            h2_lo(7)

            taps_ff = vec[:, V_FC:NV].rearrange("p (k f) -> p k f", k=9)

            def gate_of(i):
                dve.wait_ge(S["pe_done"], (QD + i * 2) * 4 + 8)
                dve.wait_ge(S["silu_done"], i + 1)
                if not (isinstance(i, int) and i == 0):
                    dve.wait_ge(S["act_ready"], i)
                sg_(dve.tensor_tensor(a32[:, :, :], ps[:, 2:4, 0:T], cv[:, :, :], ALU.mult), "act_f32")

            def act_lo_of(i):
                dve.wait_ge(S["act_h"], i + 1)
                sg_(dve.tensor_tensor(act_lo[:, bass.ds(i * 2, 2), :], a32[:, :, :],
                                      act_hi[:, bass.ds(i * 2, 2), :].bitcast(F32), ALU.subtract), "act_ready")

            K_OWN = 18
            before = own.n

            def conv(i, base):
                c = Own(dve, S["dve_own"], base)
                c(dve.tensor_copy(cwi[:, :, :], taps_ff[:, :, bass.ds(i * 2, 2)]))
                c.wait()
                dve.wait_ge(S["a_evac"], i * 2 + 2)
                img = [cv[:, j, :].rearrange("p (y x) -> p y x", y=4) for j in range(2)]
                for j in range(2):
                    c(dve.tensor_scalar(img[j], ap[:, j, :, 1:65], cwi[:, 4, j:j + 1], None, ALU.mult))
                order = [k for k in range(9) if k != 4]
                for k in order:
                    dy, dx = k // 3 - 1, k % 3 - 1
                    y0, y1 = max(0, -dy), 4 - max(0, dy)
                    for j in range(2):
                        c.wait(1)
                        ins = dve.scalar_tensor_tensor(img[j][:, y0:y1, :], ap[:, j, y0 + dy:y1 + dy, 1 + dx:65 + dx],
                                                       cwi[:, k, j:j + 1], img[j][:, y0:y1, :], ALU.mult, ALU.add)
                        if (k, j) == (8, 1):
                            sg_(ins, "conv_done")
                        else:
                            c(ins)
                assert c.n == K_OWN, c.n

            def gate_piece(i):
                dve.wait_ge(S["gate_used"], i)
                sg_(dve.tensor_copy(gsc[:, :], sc[:, 0, bass.ds(i - 1, 1)]), "gate_scale")
                dve.wait_ge(S["gate_scale"], i)
                dve.wait_ge(S["gate_in"], i * 16)
                sg_(dve.scalar_tensor_tensor(gacc[:, :], graw[:, :], gsc[:, 0:1], gacc[:, :], ALU.mult, ALU.add), "gate_used")

            def up_body(i, first, piece):
                q = QD + i * 2
                for s in range(4 if first else 0, 8):
                    if s % 4 != 3:
                        rest_sub(dve, q, s)
                    if s == 2 and not first:
                        gate_of(i - 1)
                    if s == 4 and not first:
                        act_lo_of(i - 1)
                    if s == 5 and piece:
                        gate_piece(i)
                    if s == 6:
                        conv(i, i * K_OWN + before)

            up_body(0, True, False)
            up_body(1, False, True)
            with dve.Fori(2, NGATE + 1) as i:
                up_body(i, False, True)
            with dve.Fori(NGATE + 1, NUP) as i:
                up_body(i, False, False)
            gate_of(NUP - 1)
            act_lo_of(NUP - 1)

            def fin_mul(g, eng):
                cs = slice(512 * g, 512 * g + 512)
                eng.wait_ge(S["ssf"], 2 * g + 2)
                for t in range(2):
                    eng.tensor_tensor(xm[:, t, cs], xm[:, t, cs], gfin[:, cs], ALU.mult).then_inc(S["xg"], 1)

            def dn_out(g):
                if g < 2:
                    dve.wait_ge(S["dn_evac"], 2 * g + 2)
                    src = lambda t: dr[:, g, t, :]
                else:
                    dve.wait_ge(S["pe_done"], 4 * QE + 22 * (g + 1))
                    src = lambda t: ps[:, 2 * (g % 2) + t, :]
                residual(g, gfb, src, ft_, "dn_mul", "dn_sum", 2 * g)

            for l in range(88):
                if l % 4 != 3:
                    rest_sub(dve, QE, l)
                if l == 4:
                    dve.wait_ge(S["gf_ps"], 1)
                    dve.wait_ge(S["gf_bias"], 16)
                    sg_(dve.tensor_tensor(gfb[:, :], ps[:, 4:8, :].rearrange("p a b -> p (a b)"), gfb[:, :], ALU.add), "gf_ready")
                    dve.wait_ge(S["gf_ready"], 1)
                if l in (46, 52, 70):
                    dn_out({46: 0, 52: 1, 70: 2}[l])
            dn_out(3)
            fin_mul(3, dve)
            sg_(dve.tensor_reduce(rs[:, 2:4], ss3[:, :].rearrange("p (t g) -> p t g", t=2), AXX, ALU.add), "rsum")
            dve.wait_ge(S["rstd3"], 1)
            sg_(dve.reciprocal(rs[:, 2:4], rs[:, 2:4]), "rinv")
            dve.wait_ge(S["rinv"], 1)
            dve.wait_ge(S["xg"], 8)
            sg_(dve.tensor_scalar(xm[:, 1, :], xm[:, 1, :], rs[:, 3:4], None, ALU.mult), "fin1")

        @block.gpsimd
        def _(pool):
            def sg_(ins, sem):
                ins.then_inc(S[sem], 1)

            sg_(pool.memset(pack[:, 0, :], 0.0), "row0")
            sg_(pool.memset(cvec[:, :, :].bitcast(F32), 0.0), "cv_zero")
            for l in range(3, 64, 4):
                rest_sub(pool, QA, l)
                if l == 19:
                    pool.wait_ge(S["h3_sb"], 4)
                    sg_(pool.memset(taps[0:1, 0, HYW:2 * HYW], 0.0), "row0")
                    pool.wait_ge(S["row0"], 2)

            PSTEP = {(4, 3): (0, 0), (7, 3): (0, 1), (8, 3): (0, 2), (10, 3): (1, 0), (G_Q, 3): (1, 1), (G_Q + 1, 3): (1, 2)}

            def hyena(h, step):
                if step == 0:
                    pool.wait_ge(S["hy_evac"], 20 if h else 8)
                    sg_(pool.tensor_tensor(bv[:, :, :], bv[:, :, :], bx1[:, :, :], ALU.mult), "z_done")
                if step == 1:
                    pool.wait_ge(S["y2_done"], 4 * (h + 1))
                    pool.wait_ge(S["hy_evac"], 24 if h else 12)
                    sg_(pool.tensor_tensor(bv[:, :, :], bv[:, :, :], bx0[:, :, :], ALU.mult), "y3_done")
                if step == 2:
                    pool.wait_ge(S["hy_hi"], h + 1)
                    sg_(pool.tensor_tensor(hm_lo[:, 4 * h:4 * h + 4, :], bv[:, :, :],
                                           hm_hi[:, 4 * h:4 * h + 4, :].bitcast(F32), ALU.subtract), "hy_mix")

            def gla(slot):
                p, k = divmod(slot, 5)
                if k == 0 and p < 4:
                    pool.wait_ge(S["exps"], 4 * p + 4)
                    cs = slice(P * p, P * p + P)
                    for d in range(2):
                        sg_(pool.tensor_tensor(kd[:, d, :, :], kd[:, d, :, :], ktok[:, 0:2, cs], ALU.mult), "kdc")
                        sg_(pool.tensor_tensor(kc[:, d, :, :], kc[:, d, :, :], ktok[:, 2:4, cs], ALU.mult), "kdc")
                if slot - 1 in PROD:
                    p = PROD[slot - 1]
                    pool.wait_ge(S["g_hi"], p + 1)
                    sg_(pool.tensor_tensor(gm_lo[:, 2 * p:2 * p + 2, :], sg[:, 2 * p:2 * p + 2, :],
                                           gm_hi[:, 2 * p:2 * p + 2, :].bitcast(F32), ALU.subtract), "g_mix")

            for G in range(NGRP):
                for s in range(subs_of(G)):
                    if (G, s) == (0, 0):
                        rest_sub(pool, QB, 3)
                    if G == 0:
                        for t in range(4 * s + 1, 4 * s + 4, 2):
                            pool.wait_ge(S["hx_f32"], t // 2 + 1)
                            pool.wait_ge(S["hx_hi_ready"], t + 1)
                            sg_(pool.tensor_tensor(hx_lo[:, t, :], hf[:, 1, :], hx_hi[:, t, :].bitcast(F32), ALU.subtract), "hx_pool")
                    if s % 4 == 3 and G > 0:
                        rest_sub(pool, quad_of(G), s, 128 if G == G_R else 1024)
                    if (G, s) in PSTEP:
                        hyena(*PSTEP[G, s])
                    if (G, s) == (G_R, 3):
                        pool.wait_ge(S["cplx"], 2)
                        sg_(pool.memset(wg[:, :, :], 0.0), "wg_zero")
                        pool.wait_ge(S["wg_zero"], 1)
                        sg_(pool.memset(rT[32:33, :], 1.0), "rT_one")
                        pool.wait_ge(S["rT_one"], 1)
                    if G >= G_G:
                        gla(4 * (G - G_G) + s)
            for g in range(4):
                for s in range(8):
                    if s % 4 == 3:
                        rest_sub(pool, QC + 2 * g, s)
                    if g == 0:
                        gla(16 + s)
            rest_sub(pool, QD, 3)
            pool.wait_ge(S["ssm"], 8)
            sg_(pool.memset(ap[:, :, :, :], 0.0), "ap_zero")
            pool.wait_ge(S["pe_done"], 4 * QD)
            sg_(pool.memset(gacc[:, :], 0.0), "gate_used")
            rest_sub(pool, QD, 7)
            with pool.Fori(1, NUP) as i:
                rest_sub(pool, QD + i * 2, 3)
                rest_sub(pool, QD + i * 2, 7)
            for l in range(3, 88, 4):
                rest_sub(pool, QE, l)
                if l in (51, 59, 79):
                    g = {51: 0, 59: 1, 79: 2}[l]
                    cs = slice(512 * g, 512 * g + 512)
                    pool.wait_ge(S["gfin_in"], 16)
                    pool.wait_ge(S["ssf"], 2 * g + 2)
                    for t in range(2):
                        sg_(pool.tensor_tensor(xm[:, t, cs], xm[:, t, cs], gfin[:, cs], ALU.mult), "xg")


def constants():
    n = np.arange(P)
    same = (n[:, None] // CH) == (n[None, :] // CH)
    r, c = n[:, None], n[None, :]
    g = 1.0 / 16.0
    con = np.zeros((P, 10, P), np.float32)
    con[:, K_ID] = np.eye(P)
    con[:, K_MEAN] = 1.0 / P
    con[:, K_ONE] = 1.0
    con[:, K_TF] = g * (same & (r <= c))
    con[:, K_TB] = g * (same & (r >= c))
    con[:, K_SF] = g * (same & (r > c))
    con[:, K_SB] = g * (same & (r < c))
    con[:, K_SC] = g * (r > c)
    con[:, K_PC] = g * (r < c)
    con[:, K_AL] = g
    m = (np.arange(CH)[None, :] >= (n[:, None] % CH)).astype(np.int32)
    L = 2 * T
    t, f = np.arange(T)[:, None], np.arange(T)[None, :]
    ang = 2 * np.pi * ((t * f) % L) / L
    fw = np.concatenate([np.cos(ang), -np.sin(ang)], axis=1)
    fw[:, T] = (-1.0) ** np.arange(T)
    iv = np.concatenate([2 * np.cos(ang.T), -2 * np.sin(ang.T)], axis=0) / L
    iv[0] = 1.0 / L
    iv[T] = ((-1.0) ** np.arange(T)) / L
    pos = np.arange(T)
    tn = pos / (T - 1)
    a2 = (2 * np.pi / T) * ((pos[:, None] * np.arange(1, BANDS + 1)[None, :]) % T)
    z = np.concatenate([tn[:, None], np.cos(a2), np.sin(a2)], axis=1)
    deltas = np.abs(np.linspace(np.log(1e-2) / 1.5, np.log(1e-2) / 0.3, HYW))
    dec = np.exp(-tn[:, None] * deltas[None, :])

    def tiles(x):
        return np.ascontiguousarray(x.reshape(-1, P, x.shape[1]).transpose(1, 0, 2).reshape(P, -1), np.float32)

    return {
        "con": con.reshape(P, -1), "mask": np.tile(m, (1, 2)), "sel": np.array([[1, 0], [1, 0], [0, 1], [0, 1]], np.float32),
        "fwd": tiles(fw), "inv": tiles(iv), "decay": tiles(dec), "zfeat": np.ascontiguousarray(z.T, np.float32),
    }


NAMES = ["x", "c", "ctx", "c_ctx", "w_mod", "b_mod", "g_attn", "w_in", "hy_conv", "hy_w1", "hy_b1", "hy_freq", "hy_w2", "hy_b2",
         "hy_w3", "hy_bias", "hy_out_g", "gla_wg_f", "gla_bg_f", "gla_wg_b", "gla_bg_b", "gla_out_g", "w_out", "g_ffn",
         "ffn_w_up", "ffn_conv", "ffn_w_down", "g_final"]


def kernel(**inputs):
    import concourse.bacc as bacc
    from concourse.bass_utils import run_bass_kernel_spmd

    nc = bacc.Bacc("TRN2", target_bir_lowering=False, num_devices=1)
    data = {k: np.ascontiguousarray(inputs[k]) for k in NAMES}
    data.update(constants())
    arrays, aps = {}, {}
    for k, v in data.items():
        arrays[f"in_{k}"] = v
        aps[k] = nc.dram_tensor(f"in_{k}", v.shape, mybir.dt.from_np(v.dtype), kind="ExternalInput").ap()
    out = nc.dram_tensor("out_0", (1, T, D), F32, kind="ExternalOutput").ap()
    build(nc, aps, out)
    return run_bass_kernel_spmd(nc, [arrays], core_ids=[0]).results[0]["out_0"]
```
